# Optimizing a Trainium2 kernel written in Bass

```python
import jax, jax.numpy as jnp
from jax import lax
import numpy as np

D_MODEL = 1024
BATCH = 1
SEQ = 1024
DEPTH = 2

N_MIXERS = 2
CONV_WIDTH = 3
CONV_GROUPS = 16
FOURIER_GROUPS = 8
FOURIER_GROUP_DIM = D_MODEL // FOURIER_GROUPS
D_FF = ((8 * D_MODEL // 3 + 255) // 256) * 256
N_CONV_LAYERS = (DEPTH + 1) // 2
N_FOURIER_LAYERS = DEPTH // 2
RMS_EPS = 1e-5

kernel_name = "hybrid_shortconv_fourier_encoder"

def rmsnorm(x, g):
    xf = x.astype(jnp.float32)
    r = lax.rsqrt(jnp.mean(xf * xf, axis=-1, keepdims=True) + RMS_EPS)
    return (xf * r * g.astype(jnp.float32)).astype(x.dtype)

def short_conv_mixer(h, w_in, k, w_out):
    bcv = jnp.einsum('bsd,de->bse', h, w_in)
    gate_b, gate_c, v = jnp.split(bcv, 3, axis=-1)
    u = gate_c * v
    up = jnp.pad(u, ((0, 0), (1, 1), (0, 0)))
    conv = k[0] * up[:, :-2] + k[1] * up[:, 1:-1] + k[2] * up[:, 2:]
    return jnp.einsum('bsd,de->bse', gate_b * conv, w_out)

def fourier_mixer(h, w_out):
    bsz, seq, dm = h.shape
    hf = h.astype(jnp.float32).reshape(bsz, seq, FOURIER_GROUPS, FOURIER_GROUP_DIM)
    f = jnp.fft.fft2(hf, axes=(1, 3), norm='ortho')
    y = jnp.real(f).astype(h.dtype).reshape(bsz, seq, dm)
    return jnp.einsum('bsd,de->bse', y, w_out)

def swiglu(h, w_gate, w_up, w_down):
    a = jnp.einsum('bsd,df->bsf', h, w_gate)
    b = jnp.einsum('bsd,df->bsf', h, w_up)
    return jnp.einsum('bsf,fd->bsd', jax.nn.silu(a) * b, w_down)

def setup_inputs(seed: int = 0) -> dict:
    key = jax.random.key(seed)
    ks = jax.random.split(key, 12)
    f32 = jnp.float32
    x = jax.random.normal(ks[0], (BATCH, SEQ, D_MODEL), f32)
    conv_w_in = jax.random.normal(ks[1], (N_CONV_LAYERS, D_MODEL, 3 * D_MODEL), f32) * D_MODEL ** -0.5
    conv_k = jax.random.normal(ks[2], (N_CONV_LAYERS, CONV_WIDTH, D_MODEL), f32) * CONV_WIDTH ** -0.5
    conv_w_out = jax.random.normal(ks[3], (N_CONV_LAYERS, D_MODEL, D_MODEL), f32) * D_MODEL ** -0.5
    fourier_w_out = jax.random.normal(ks[4], (N_FOURIER_LAYERS, D_MODEL, D_MODEL), f32) * D_MODEL ** -0.5
    mix_norm_g = 1.0 + 0.02 * jax.random.normal(ks[5], (DEPTH, D_MODEL), f32)
    ffn_norm_g = 1.0 + 0.02 * jax.random.normal(ks[6], (DEPTH, D_MODEL), f32)
    ffn_w_gate = jax.random.normal(ks[7], (DEPTH, D_MODEL, D_FF), f32) * D_MODEL ** -0.5
    ffn_w_up = jax.random.normal(ks[8], (DEPTH, D_MODEL, D_FF), f32) * D_MODEL ** -0.5
    ffn_w_down = jax.random.normal(ks[9], (DEPTH, D_FF, D_MODEL), f32) * D_FF ** -0.5
    final_norm_g = 1.0 + 0.02 * jax.random.normal(ks[10], (D_MODEL,), f32)
    return {
        'x': x,
        'conv_w_in': conv_w_in,
        'conv_k': conv_k,
        'conv_w_out': conv_w_out,
        'fourier_w_out': fourier_w_out,
        'mix_norm_g': mix_norm_g,
        'ffn_norm_g': ffn_norm_g,
        'ffn_w_gate': ffn_w_gate,
        'ffn_w_up': ffn_w_up,
        'ffn_w_down': ffn_w_down,
        'final_norm_g': final_norm_g,
    }

def reference(x, conv_w_in, conv_k, conv_w_out, fourier_w_out, mix_norm_g,
              ffn_norm_g, ffn_w_gate, ffn_w_up, ffn_w_down, final_norm_g):
    h = x
    for i in range(DEPTH):
        hn = rmsnorm(h, mix_norm_g[i])
        j = i // N_MIXERS
        if i % N_MIXERS == 0:
            h = h + short_conv_mixer(hn, conv_w_in[j], conv_k[j], conv_w_out[j])
        else:
            h = h + fourier_mixer(hn, fourier_w_out[j])
        hn = rmsnorm(h, ffn_norm_g[i])
        h = h + swiglu(hn, ffn_w_gate[i], ffn_w_up[i], ffn_w_down[i])
    return rmsnorm(h, final_norm_g)


_drawn_inputs = setup_inputs


def setup_inputs(seed=0):
    import zlib

    import numpy as np

    out = dict(_drawn_inputs(seed))
    spreads = {}
    factors = {'ffn_norm_g': 3.653, 'final_norm_g': 2.927}
    for name, (base, spread) in spreads.items():
        noise = np.random.default_rng([zlib.crc32(name.encode()), seed]).standard_normal(out[name].shape)
        drawn = base * np.exp(spread * noise) if base else spread * noise
        out[name] = __import__('jax').numpy.asarray(drawn.astype(out[name].dtype))
    for name, factor in factors.items():
        out[name] = (out[name] * factor).astype(out[name].dtype)
    return out
```

```python
import concourse.bass as bass
from concourse import mybir
from contextlib import ExitStack

P = 128
D = 1024
S = 1024
KC = D // P
HALF = 512
FF = 2816
FC = FF // P
FG = FC // 2
CG = KC // 2
RMS_EPS = 1e-5
RAW = 3
RING = 6
ACTS = 4
BANKS = 4
UNITS_IN_PAIR = 12

CONV_U = 0
FFN_U = [CONV_U + 4 * KC, 0]
FOUR_U = FFN_U[0] + 3 * FC
FFN_U[1] = FOUR_U + 4 + KC
CONV_Q = 0
FFN_Q = [3 * KC, 3 * KC + 2 * FC + KC]
FOUR_Q = FFN_Q[0] + 2 * FC
CONV_N = 0
FFN_N = [16 * CG, 16 * (CG + FG)]
CONV_A = 0
FFN_A = [KC, KC + FC]
NORM_CONV, NORM_FFN0, NORM_FOUR, NORM_FFN1, NORM_FINAL = range(5)


def conv_in_unit(g):
    return CONV_U + (0 if g == 0 else 8 * g - 2)


def conv_down_unit(g):
    return CONV_U + (8 * g + 12 if g < CG - 1 else 4 * KC - 2)


def ffn_in_unit(layer, g):
    return g * 6 + (FFN_U[layer] - 2)


def ffn_down_unit(layer, g):
    return g * 6 + (FFN_U[layer] + 8)


def build(nc, xT, w_in, w_conv, w_four, w_gate, w_up, w_down, gains_d, taps_d, seq_d, feat_d, cst_d, outT):
    F32 = mybir.dt.float32
    F32R = mybir.dt.float32r
    ALU = mybir.AluOpType
    ACT = mybir.ActivationFunctionType

    ctx = ExitStack()
    with ctx:
        def sb(name, shape, dt=F32):
            return ctx.enter_context(nc.sbuf_tensor(name, shape, dt))

        def sem(name):
            return ctx.enter_context(nc.semaphore(name))

        res = sb("res", [P, KC, S])
        xs_h = sb("xs_h", [P, KC, S], F32R)
        xs_l = sb("xs_l", [P, KC, S], F32R)
        mid_h = sb("mid_h", [P, ACTS, S], F32R)
        mid_l = sb("mid_l", [P, ACTS, S], F32R)
        raw = sb("raw", [P, RAW, D])
        ring_h = sb("ring_h", [P, RING, D], F32R)
        ring_l = sb("ring_l", [P, RING, D], F32R)
        t_a = sb("t_a", [P, S])
        t_b = sb("t_b", [P, S])
        padded = sb("padded", [P, S + 2])
        acc = padded[:, 1:S + 1]
        rb = sb("rb", [P, S])
        gains = sb("gains", [P, 5, KC])
        taps = sb("taps", [P, 3, KC])
        cst = sb("cst", [P, P + 2])
        ident = cst[:, 0:P]
        ones = sb("ones", [P, P])
        feat_h = sb("feat_h", [P, 2 * P], F32R)
        feat_l = sb("feat_l", [P, 2 * P], F32R)
        alt = sb("alt", [P, 2], F32R)
        stat = sb("stat", [P, KC])
        rcol = sb("rcol", [P, KC])

        pin = ctx.enter_context(nc.psum_tensor("pin", [P, 4, HALF], F32))
        pdn = ctx.enter_context(nc.psum_tensor("pdn", [P, BANKS, HALF], F32))

        raw_landed = [sem(f"raw_landed{i}") for i in range(RAW)]
        unit_high = sem("unit_high")
        unit_ready = sem("unit_ready")
        unit_used = sem("unit_used")
        x_landed = [sem(f"x_landed{i}") for i in range(KC)]
        small_landed = sem("small_landed")
        feat_landed = sem("feat_landed")
        feat_high = sem("feat_high")
        feat_ready = sem("feat_ready")
        ones_set = sem("ones_set")
        alt_ready = sem("alt_ready")
        edges_set = sem("edges_set")
        xs_high = sem("xs_high")
        xs_ready = sem("xs_ready")
        sq_done = sem("sq_done")
        acc_done = sem("acc_done")
        colsum_done = sem("colsum_done")
        stat_done = sem("stat_done")
        root_done = sem("root_done")
        rcol_ready = sem("rcol_ready")
        diag_done = sem("diag_done")
        bcast_done = sem("bcast_done")
        rb_ready = sem("rb_ready")
        in_done = sem("in_done")
        in_free = sem("in_free")
        gate2 = sem("gate2")
        tap_mid = sem("tap_mid")
        tap_left = sem("tap_left")
        tap_right = sem("tap_right")
        silu_done = sem("silu_done")
        mid_made = sem("mid_made")
        mid_high = sem("mid_high")
        mid_ready = sem("mid_ready")
        down_done = sem("down_done")
        down_added = sem("down_added")
        z_done = sem("z_done")
        z_lo = sem("z_lo")
        z_hi = sem("z_hi")
        plus_made = sem("plus_made")
        minus_made = sem("minus_made")
        plus_high = sem("plus_high")
        minus_high = sem("minus_high")
        fold_ready = sem("fold_ready")
        y_done = sem("y_done")
        y_cos = sem("y_cos")
        y_made = sem("y_made")
        y_high = sem("y_high")
        y_ready = sem("y_ready")
        scaled = sem("scaled")
        stored = sem("stored")

        block = ctx.enter_context(nc.Block())

        @block.sync
        def _(sp):
            def load_unit(u, slot_of, src):
                if not isinstance(u, int) or u >= RAW:
                    sp.wait_ge(unit_ready, u - (RAW - 1))
                sp.dma_start(raw[:, slot_of % RAW, :], src).then_inc(raw_landed[slot_of % RAW], 16)

            def col_rows(w, f):
                return w[bass.ds(f * P, P), :]

            def conv_in(g):
                u = conv_in_unit(g)
                for j in range(2):
                    for part in (1, 2, 0):
                        load_unit(u, u, col_rows(w_in, part * KC + 2 * g + j))
                        u += 1

            def conv_down(g):
                for j in range(2):
                    u = conv_down_unit(g) + j
                    load_unit(u, u, col_rows(w_conv, 2 * g + j))

            def ffn_in(layer, g, u, slot):
                for j in range(2):
                    for w in (w_gate, w_up):
                        load_unit(u, slot, col_rows(w, g * 2 + (layer * FC + j)))
                        u, slot = u + 1, slot + 1

            def ffn_down(layer, g, u, slot):
                for j in range(2):
                    load_unit(u + j, slot + j, col_rows(w_down, g * 2 + (layer * FC + j)))

            def ffn(layer):
                ffn_in(layer, 0, FFN_U[layer], FFN_U[layer])
                with sp.Fori(0, (FG - 1) // 2) as i:
                    for odd in (1, 2):
                        g = i * 2 + odd
                        ffn_in(layer, g, ffn_in_unit(layer, g), FFN_U[layer] - 2 + 6 * odd)
                        ffn_down(layer, g - 1, ffn_down_unit(layer, g - 1), FFN_U[layer] + 2 + 6 * odd)
                last = FFN_U[layer] + 3 * FC - 2
                ffn_down(layer, FG - 1, last, last)

            sp.dma_start(res[:, 0, :], xT[0:P, :]).then_inc(x_landed[0], 16)
            load_unit(0, 0, col_rows(w_in, KC))
            for m in range(1, KC):
                sp.dma_start(res[:, m, :], xT[m * P:(m + 1) * P, :]).then_inc(x_landed[m], 16)
            for g in range(CG):
                if g == 0:
                    u = 1
                    for j in range(2):
                        for part in (1, 2, 0):
                            if (j, part) != (0, 1):
                                load_unit(u, u, col_rows(w_in, part * KC + j))
                                u += 1
                else:
                    conv_in(g)
                    conv_down(g - 1)
            conv_down(CG - 1)
            ffn(0)
            for t in range(4):
                load_unit(FOUR_U + t, FOUR_U + t, seq_d[t * P:(t + 1) * P, :])
            for m in range(KC):
                load_unit(FOUR_U + 4 + m, FOUR_U + 4 + m, col_rows(w_four, m))
            ffn(1)
            for h in range(2):
                for m in range(KC):
                    sp.wait_ge(scaled, h * KC + m + 1)
                    sp.dma_start(outT[m * P:(m + 1) * P, h * HALF:(h + 1) * HALF],
                                 res[:, m, h * HALF:(h + 1) * HALF]).then_inc(stored, 16)
            sp.wait_ge(stored, 16 * 2 * KC)

        @block.gpsimd
        def _(pool):
            def split_unit(u, slot_of, landed):
                pool.wait_ge(raw_landed[slot_of % RAW], landed * 16)
                if not isinstance(u, int) or u >= RING:
                    pool.wait_ge(unit_used, u - (RING - 1))
                src = raw[:, slot_of % RAW, :]
                high = ring_h[:, slot_of % RING, :]
                if isinstance(u, int):
                    nc.gpsimd.tensor_copy(high, src).then_inc(unit_high, 1)
                else:
                    blocks = [ap.rearrange("p (c n) -> p c n", n=P) for ap in (high, src)]
                    one = ones[:].rearrange("p (c n) -> p c n", c=1).to_broadcast([P, KC, P])
                    nc.gpsimd.tensor_tensor(blocks[0], blocks[1], one, ALU.mult).then_inc(unit_high, 1)
                pool.wait_ge(unit_high, u + 1)
                nc.gpsimd.tensor_tensor(ring_l[:, slot_of % RING, :], src, high.bitcast(F32),
                                        ALU.subtract).then_inc(unit_ready, 1)

            def split_units(first, end):
                for u in range(first, end):
                    split_unit(u, u, u // RAW + 1)

            def add_square(norm, m):
                pool.wait_ge(sq_done, norm * KC + m + 1)
                if m >= 2:
                    pool.wait_ge(acc_done, norm * (KC - 1) + m - 1)
                sq = t_a if m % 2 else t_b
                nc.gpsimd.tensor_tensor(acc, acc, sq[:], ALU.add).then_inc(acc_done, 1)

            def ffn(layer):
                first = FFN_U[layer] + 4
                with pool.Fori(0, (FG - 1) // 2) as i:
                    for j in range(UNITS_IN_PAIR):
                        u = first + j
                        split_unit(i * UNITS_IN_PAIR + u, u, i * (UNITS_IN_PAIR // RAW) + (u // RAW + 1))
                split_units(FFN_U[layer] + 3 * FC - 2, FFN_U[layer] + 3 * FC)

            nc.gpsimd.memset(ones[:], 1.0).then_inc(ones_set, 1)
            nc.gpsimd.memset(padded[:, 0:1], 0.0).then_inc(edges_set, 1)
            nc.gpsimd.memset(padded[:, S + 1:S + 2], 0.0).then_inc(edges_set, 1)
            split_units(0, 1)
            for m in range(1, KC):
                add_square(NORM_CONV, m)
                if m == 3:
                    split_units(1, 2)
                if m == 6:
                    pool.wait_ge(feat_landed, 16)
                    nc.gpsimd.tensor_copy(feat_h[:], rb[:, 0:2 * P]).then_inc(feat_high, 1)
                    pool.wait_ge(feat_high, 1)
                    nc.gpsimd.tensor_tensor(feat_l[:], rb[:, 0:2 * P], feat_h[:].bitcast(F32),
                                            ALU.subtract).then_inc(feat_ready, 1)
            split_units(2, FFN_U[0] + 4)
            for m in range(1, KC):
                add_square(NORM_FFN0, m)
            ffn(0)
            split_units(FOUR_U, FOUR_U + 4)
            for m in range(1, KC):
                add_square(NORM_FOUR, m)
            split_units(FOUR_U + 4, FOUR_U + 6)
            for g in range(KC):
                pool.wait_ge(y_high, g + 1)
                nc.gpsimd.tensor_tensor(xs_l[:, g, :], rb[:], xs_h[:, g, :].bitcast(F32),
                                        ALU.subtract).then_inc(y_ready, 1)
            split_units(FOUR_U + 6, FOUR_U + 10)
            for m in range(KC):
                if m:
                    add_square(NORM_FFN1, m)
                if m < 6:
                    split_units(FOUR_U + 10 + m, FOUR_U + 11 + m)
            ffn(1)
            for h in range(2):
                for m in range(1, KC):
                    pool.wait_ge(sq_done, NORM_FINAL * KC + h * KC + m + 1)
                    if m >= 2:
                        pool.wait_ge(acc_done, (NORM_FINAL + h) * (KC - 1) + m - 1)
                    sq = t_a if m % 2 else t_b
                    cols = slice(h * HALF, (h + 1) * HALF)
                    nc.gpsimd.tensor_tensor(acc[:, cols], acc[:, cols], sq[:, cols],
                                            ALU.add).then_inc(acc_done, 1)

        @block.scalar
        def _(act):
            def norm_high(norm, m):
                nc.scalar.activation(xs_h[:, m, :], res[:, m, :], ACT.Copy,
                                     scale=gains[:, norm, m:m + 1]).then_inc(xs_high, 1)

            def norm_square(norm, m):
                if m >= 3:
                    act.wait_ge(acc_done, norm * (KC - 1) + m - 2)
                sq = acc if m == 0 else t_a[:] if m % 2 else t_b[:]
                nc.scalar.activation(sq, res[:, m, :], ACT.Square).then_inc(sq_done, 1)

            def norm_feed(norm, wait_chunk):
                for m in range(KC):
                    wait_chunk(m)
                    norm_high(norm, m)
                    norm_square(norm, m)

            def norm_root(k, c0, c1):
                act.wait_ge(stat_done, k + 1)
                nc.scalar.activation(stat[:, c0:c1], stat[:, c0:c1], ACT.Sqrt).then_inc(root_done, 1)

            def norm_spread(k, c0, c1):
                act.wait_ge(bcast_done, k)
                n = (c1 - c0) // HALF
                nc.scalar.activation(rb[:, c0:c1], pdn[:, 1:1 + n, :], ACT.Copy).then_inc(rb_ready, 1)

            def mid_round(a, slot):
                act.wait_ge(mid_made, a + 1)
                nc.scalar.activation(mid_h[:, slot, :], t_b[:], ACT.Copy).then_inc(mid_high, 1)

            def conv_chunk(f):
                act.wait_ge(in_free, 3 * f + 2)
                nc.scalar.activation(t_a[:], acc, ACT.Copy, scale=taps[:, 1, f:f + 1]).then_inc(tap_mid, 1)
                mid_round(f, f % ACTS)

            def ffn_group(layer, g, odd):
                for j in range(2):
                    act.wait_ge(in_free, g * 4 + (FFN_Q[layer] + 2 * j + 1))
                    nc.scalar.activation(t_a[:], t_a[:], ACT.Silu).then_inc(silu_done, 1)
                    mid_round(g * 2 + (FFN_A[layer] + j), 2 * (odd % 2) + j)

            def ffn(layer):
                ffn_group(layer, 0, 0)
                with act.Fori(0, (FG - 1) // 2) as i:
                    for odd in (1, 2):
                        ffn_group(layer, i * 2 + odd, odd)

            def last_down(base, norm):
                def wait_chunk(m):
                    act.wait_ge(down_added, base + 2 * m + 2)
                norm_feed(norm, wait_chunk)

            act.dma_start(gains[:], gains_d).then_inc(small_landed, 16)
            act.dma_start(taps[:], taps_d).then_inc(small_landed, 16)
            act.dma_start(cst[:], cst_d).then_inc(small_landed, 16)
            act.dma_start(rb[:, 0:2 * P], feat_d).then_inc(feat_landed, 16)
            act.wait_ge(small_landed, 16 * 3)
            nc.scalar.activation(alt[:], cst[:, P:P + 2], ACT.Copy).then_inc(alt_ready, 1)
            norm_feed(NORM_CONV, lambda m: act.wait_ge(x_landed[m], 16))
            norm_root(NORM_CONV, 0, KC)
            act.wait_ge(feat_ready, 1)
            norm_spread(NORM_CONV + 1, 0, S)
            for f in range(KC):
                conv_chunk(f)
            act.wait_ge(mid_ready, CONV_A + KC)
            last_down(CONV_N + 16 * (CG - 1), NORM_FFN0)
            norm_root(NORM_FFN0, 0, KC)
            norm_spread(NORM_FFN0 + 1, 0, S)
            ffn(0)
            act.wait_ge(mid_ready, FFN_A[0] + FC)
            last_down(FFN_N[0] + 16 * (FG - 1), NORM_FOUR)
            norm_root(NORM_FOUR, 0, KC)
            act.wait_ge(rcol_ready, NORM_FOUR + 1)

            def y_leaves(g):
                act.wait_ge(y_done, g + 1)
                if g:
                    act.wait_ge(y_ready, g)
                nc.scalar.activation(rb[:, 0:HALF].rearrange("p (j e) -> p j e", e=2),
                                     pdn[:, 2 * (g % 2), :].rearrange("p (e j) -> p j e", e=2),
                                     ACT.Copy).then_inc(y_cos, 1)
                act.wait_ge(y_made, g + 1)
                nc.scalar.activation(xs_h[:, g, :], rb[:], ACT.Copy).then_inc(y_high, 1)

            for g in range(KC):
                act.wait_ge(z_done, 2 * g + 1)
                if g:
                    act.wait_ge(fold_ready, 2 * g)
                for c in range(4):
                    last = nc.scalar.activation(t_a[:, c * 256:(c + 1) * 256],
                                                pin[:, c // 2, (c % 2) * 256:(c % 2 + 1) * 256],
                                                ACT.Copy, scale=rcol[:, c:c + 1])
                last.then_inc(z_lo, 1)
                act.wait_ge(plus_made, g + 1)
                nc.scalar.activation(mid_h[:, 2 * (g % 2), :], acc, ACT.Copy).then_inc(plus_high, 1)
                act.wait_ge(minus_made, g + 1)
                nc.scalar.activation(mid_h[:, 2 * (g % 2) + 1, :], t_a[:], ACT.Copy).then_inc(minus_high, 1)
                if g:
                    y_leaves(g - 1)
            y_leaves(KC - 1)

            for m in range(KC):
                act.wait_ge(in_free, FOUR_Q + m + 1)
                norm_square(NORM_FFN1, m)
            act.wait_ge(in_done, FOUR_Q + KC)
            for m in range(KC):
                norm_high(NORM_FFN1, m)
            norm_root(NORM_FFN1, 0, KC)
            norm_spread(NORM_FFN1, 0, S)
            ffn(1)
            def final_squares(h, first, end):
                cols = slice(h * HALF, (h + 1) * HALF)
                for m in range(first, end):
                    act.wait_ge(down_added, FFN_N[1] + 16 * (FG - 1) + KC * h + m + 1)
                    if m >= 3:
                        act.wait_ge(acc_done, (NORM_FINAL + h) * (KC - 1) + m - 2)
                    sq = acc if m == 0 else t_a if m % 2 else t_b
                    nc.scalar.activation(sq[:, cols], res[:, m, cols], ACT.Square).then_inc(sq_done, 1)

            def final_spread(h):
                act.wait_ge(bcast_done, NORM_FINAL + h)
                nc.scalar.activation(rb[:, h * HALF:(h + 1) * HALF], pin[:, 2 * h + 1, :],
                                     ACT.Copy).then_inc(rb_ready, 1)

            act.wait_ge(mid_ready, FFN_A[1] + FC)
            final_squares(0, 0, KC)
            final_squares(1, 0, 4)
            norm_root(NORM_FINAL, 0, 4)
            final_squares(1, 4, 6)
            final_spread(0)
            final_squares(1, 6, KC)
            norm_root(NORM_FINAL + 1, 4, 8)
            final_spread(1)

        @block.vector
        def _(dve):
            def norm_low(norm, m):
                dve.wait_ge(xs_high, norm * KC + m + 1)
                nc.vector.scalar_tensor_tensor(xs_l[:, m, :], res[:, m, :], gains[:, norm, m:m + 1],
                                               xs_h[:, m, :].bitcast(F32), ALU.mult,
                                               ALU.subtract).then_inc(xs_ready, 1)

            def norm_column(k, colsum, c0, c1):
                dve.wait_ge(colsum_done, k + 1)
                nc.vector.tensor_scalar(stat[:, c0:c1], colsum, 1.0 / D, RMS_EPS, ALU.mult,
                                        ALU.add).then_inc(stat_done, 1)
                dve.wait_ge(root_done, k + 1)
                nc.vector.reciprocal(rcol[:, c0:c1], stat[:, c0:c1]).then_inc(rcol_ready, 1)
                dve.wait_ge(rcol_ready, k + 1)

            def norm_diag(c0, c1):
                n = c1 - c0
                nc.vector.tensor_tensor(
                    t_a[:, c0 * P:c1 * P].rearrange("p (j n) -> p j n", n=P),
                    ident.rearrange("p (j n) -> p j n", j=1).to_broadcast([P, n, P]),
                    rcol[:, c0:c1].rearrange("p (j n) -> p j n", n=1).to_broadcast([P, n, P]),
                    ALU.mult).then_inc(diag_done, 1)

            def scale_out(q, pair, dst):
                dve.wait_ge(in_done, q + 1)
                nc.vector.tensor_tensor(dst, pin[:, 2 * pair:2 * pair + 2, :].rearrange("p b n -> p (b n)"),
                                        rb[:], ALU.mult).then_inc(in_free, 1)
                dve.wait_ge(in_free, q + 1)

            def mid_low(a, slot):
                dve.wait_ge(mid_high, a + 1)
                nc.vector.tensor_tensor(mid_l[:, slot, :], t_b[:], mid_h[:, slot, :].bitcast(F32),
                                        ALU.subtract).then_inc(mid_ready, 1)

            def down_add(n, m, h, bank):
                dve.wait_ge(down_done, n + 1)
                cols = slice(h * HALF, (h + 1) * HALF)
                nc.vector.tensor_tensor(res[:, m, cols], pdn[:, bank, :], res[:, m, cols],
                                        ALU.add).then_inc(down_added, 1)

            def down_adds(base, first, end):
                for n in range(first, end):
                    down_add(base + n, n // 2, n % 2, n % BANKS)

            def last_down(base, norm):
                for m in range(KC):
                    down_adds(base, 2 * m, 2 * m + 2)
                    if m:
                        norm_low(norm, m - 1)
                norm_low(norm, KC - 1)

            def conv_chunk(f, tail):
                q = 3 * f
                scale_out(q, q % 2, t_a[:])
                nc.vector.tensor_tensor(t_a[:], t_a[:], rb[:], ALU.mult).then_inc(gate2, 1)
                dve.wait_ge(gate2, f + 1)
                dve.wait_ge(in_done, q + 2)
                pair = (q + 1) % 2
                nc.vector.tensor_tensor(acc, pin[:, 2 * pair:2 * pair + 2, :].rearrange("p b n -> p (b n)"),
                                        t_a[:], ALU.mult).then_inc(in_free, 1)
                dve.wait_ge(in_free, q + 2)
                dve.wait_ge(tap_mid, f + 1)
                nc.vector.scalar_tensor_tensor(t_a[:], padded[:, 0:S], taps[:, 0, f:f + 1], t_a[:],
                                               ALU.mult, ALU.add).then_inc(tap_left, 1)
                dve.wait_ge(tap_left, f + 1)
                nc.vector.scalar_tensor_tensor(t_a[:], padded[:, 2:S + 2], taps[:, 2, f:f + 1], t_a[:],
                                               ALU.mult, ALU.add).then_inc(tap_right, 1)
                dve.wait_ge(tap_right, f + 1)
                scale_out(q + 2, q % 2, t_b[:])
                nc.vector.tensor_tensor(t_b[:], t_b[:], t_a[:], ALU.mult).then_inc(mid_made, 1)
                tail()
                mid_low(f, f % ACTS)

            def ffn_group(layer, g, odd, down_base):
                for j in range(2):
                    q = g * 4 + (FFN_Q[layer] + 2 * j)
                    a = g * 2 + (FFN_A[layer] + j)
                    scale_out(q, 0, t_a[:])
                    scale_out(q + 1, 1, t_b[:])
                    dve.wait_ge(silu_done, a - (KC - 1))
                    nc.vector.tensor_tensor(t_b[:], t_b[:], t_a[:], ALU.mult).then_inc(mid_made, 1)
                    if j and down_base is not None:
                        down_adds(down_base, 0, 2)
                    mid_low(a, 2 * (odd % 2) + j)
                if down_base is not None:
                    down_adds(down_base, 2, 16)

            def ffn(layer):
                ffn_group(layer, 0, 0, None)
                with dve.Fori(0, (FG - 1) // 2) as i:
                    for odd in (1, 2):
                        g = i * 2 + odd
                        ffn_group(layer, g, odd, i * 32 + (FFN_N[layer] + 16 * (odd - 1)))

            dve.wait_ge(small_landed, 16 * 3)
            dve.wait_ge(edges_set, 2)
            for m in range(KC):
                norm_low(NORM_CONV, m)
            norm_column(NORM_CONV, pdn[:, 0, 0:KC], 0, KC)
            norm_diag(0, KC)
            dve.wait_ge(rb_ready, 1)
            for f in range(KC):
                g, j = divmod(f, 2)
                adds = j == 1 and g >= 1
                conv_chunk(f, (lambda: down_adds(16 * (g - 1), 0, 2)) if adds else (lambda: None))
                if adds:
                    down_adds(16 * (g - 1), 2, 16)
            last_down(CONV_N + 16 * (CG - 1), NORM_FFN0)
            norm_column(NORM_FFN0, pdn[:, 0, 0:KC], 0, KC)
            norm_diag(0, KC)
            dve.wait_ge(rb_ready, 2)
            ffn(0)
            last_down(FFN_N[0] + 16 * (FG - 1), NORM_FOUR)
            norm_column(NORM_FOUR, pdn[:, 0, 0:KC], 0, KC)

            def y_leaves(g):
                sine = pdn[:, 2 * (g % 2) + 1, :]
                y_even = rb[:].rearrange("p (j e) -> p j e", e=2)[:, :, 0]
                y_odd = rb[:].rearrange("p (j e) -> p j e", e=2)[:, :, 1]
                Q = S // 4
                dve.wait_ge(y_cos, g + 1)
                nc.vector.tensor_tensor(y_even[:, S // 2 - 1:Q:-1], y_even[:, 1:Q], sine[:, 1:Q], ALU.add)
                nc.vector.tensor_tensor(y_odd[:, S // 2 - 1:Q - 1:-1], y_odd[:, 0:Q], sine[:, Q:2 * Q], ALU.add)
                nc.vector.tensor_tensor(y_even[:, 1:Q], y_even[:, 1:Q], sine[:, 1:Q], ALU.subtract)
                nc.vector.tensor_tensor(y_odd[:, 0:Q], y_odd[:, 0:Q], sine[:, Q:2 * Q], ALU.subtract)
                nc.vector.tensor_copy(rb[:, S // 2:S // 2 + 1], sine[:, 0:1]).then_inc(y_made, 1)

            for g in range(KC):
                dve.wait_ge(z_done, 2 * g + 2)
                nc.vector.tensor_tensor(
                    t_b[:].rearrange("p (c n) -> p c n", c=4),
                    pin[:, 2:4, :].rearrange("p b (c n) -> p (b c) n", c=2),
                    rcol[:, 4:8].rearrange("p (c n) -> p c n", n=1).to_broadcast([P, 4, 256]),
                    ALU.mult).then_inc(z_hi, 1)
                dve.wait_ge(z_hi, g + 1)
                dve.wait_ge(z_lo, g + 1)
                nc.vector.tensor_tensor(acc, t_a[:], t_b[:], ALU.add).then_inc(plus_made, 1)
                nc.vector.tensor_tensor(t_a[:], t_a[:], t_b[:], ALU.subtract).then_inc(minus_made, 1)
                dve.wait_ge(plus_made, g + 1)
                dve.wait_ge(plus_high, g + 1)
                slot = 2 * (g % 2)
                nc.vector.tensor_tensor(mid_l[:, slot, :], acc, mid_h[:, slot, :].bitcast(F32),
                                        ALU.subtract).then_inc(fold_ready, 1)
                dve.wait_ge(minus_made, g + 1)
                dve.wait_ge(minus_high, g + 1)
                nc.vector.tensor_tensor(mid_l[:, slot + 1, :], t_a[:], mid_h[:, slot + 1, :].bitcast(F32),
                                        ALU.subtract).then_inc(fold_ready, 1)
                if g:
                    y_leaves(g - 1)
            y_leaves(KC - 1)
            for m in range(KC):
                q = FOUR_Q + m
                dve.wait_ge(in_done, q + 1)
                pair = q % 2
                nc.vector.tensor_tensor(res[:, m, :], pin[:, 2 * pair:2 * pair + 2, :].rearrange("p b n -> p (b n)"),
                                        res[:, m, :], ALU.add).then_inc(in_free, 1)
            for m in range(KC):
                norm_low(NORM_FFN1, m)
            norm_column(NORM_FFN1, pdn[:, 0, 0:KC], 0, KC)
            norm_diag(0, KC)
            dve.wait_ge(rb_ready, 3)
            ffn(1)
            def final_adds(first, end):
                for n in range(first, end):
                    down_add(FFN_N[1] + 16 * (FG - 1) + n, n % KC, n // KC, n % BANKS)

            def final_scale(h, first, end):
                cols = slice(h * HALF, (h + 1) * HALF)
                for m in range(first, end):
                    nc.vector.scalar_tensor_tensor(res[:, m, cols], res[:, m, cols],
                                                   gains[:, NORM_FINAL, m:m + 1], rb[:, cols],
                                                   ALU.mult, ALU.mult).then_inc(scaled, 1)

            final_adds(0, 12)
            norm_column(NORM_FINAL, pin[:, 0, 0:4], 0, 4)
            norm_diag(0, 4)
            final_adds(12, 14)
            dve.wait_ge(rb_ready, 4)
            final_scale(0, 0, 2)
            final_adds(14, 15)
            final_scale(0, 2, 4)
            final_adds(15, 16)
            final_scale(0, 4, KC)
            norm_column(NORM_FINAL + 1, pin[:, 2, 0:4], 4, 8)
            norm_diag(4, 8)
            dve.wait_ge(rb_ready, 5)
            final_scale(1, 0, KC)

        @block.tensor
        def _(pe):

            def passes(w_h, w_l, x_h, x_l):
                return ((w_h, x_h), (w_l, x_h), (w_h, x_l))

            def project(u, slot_of, q, pair, before_chunk=None):
                slot = slot_of % RING
                pe.wait_ge(unit_ready, u + 1)
                if not isinstance(q, int) or q >= 2:
                    pe.wait_ge(in_free, q - 1)
                for k in range(KC):
                    if before_chunk is not None:
                        before_chunk(k)
                    w = slice(k * P, (k + 1) * P)
                    for h in range(2):
                        cols = slice(h * HALF, (h + 1) * HALF)
                        for i, (st, mv) in enumerate(passes(ring_h[:, slot, w], ring_l[:, slot, w],
                                                            xs_h[:, k, cols], xs_l[:, k, cols])):
                            last = nc.tensor.matmul(pin[:, 2 * pair + h, :], st, mv,
                                                    start=k == 0 and i == 0, stop=k == KC - 1 and i == 2)
                            if k == 0 and h == 0 and i == 0 and slot_of > 0:
                                last.then_inc(unit_used, 1)
                last.then_inc(in_done, 1)

            def down(u, slot_of, a, base, odd, banks=range(16), halves_outer=False):
                if banks[0] == 0:
                    pe.wait_ge(unit_ready, u + 2)
                    pe.wait_ge(mid_ready, a + 2)
                for n in banks:
                    h, m = divmod(n, KC) if halves_outer else (n % 2, n // 2)
                    if not isinstance(base, int) or base + n >= BANKS:
                        pe.wait_ge(down_added, base + (n - (BANKS - 1)))
                    w, cols = slice(m * P, (m + 1) * P), slice(h * HALF, (h + 1) * HALF)
                    for j in range(2):
                        slot, mid = (slot_of + j) % RING, 2 * (odd % 2) + j
                        for i, (st, mv) in enumerate(passes(ring_h[:, slot, w], ring_l[:, slot, w],
                                                            mid_h[:, mid, cols], mid_l[:, mid, cols])):
                            last = nc.tensor.matmul(pdn[:, n % BANKS, :], st, mv, start=j == 0 and i == 0,
                                                    stop=j == 1 and i == 2)
                            if n == 0 and j == 0 and i == 0:
                                last.then_inc(unit_used, 1)
                        if n == 15 and j == 0:
                            last.then_inc(unit_used, 1)
                    last.then_inc(down_done, 1)

            def column_sums(k, dst, c0, c1):
                pe.wait_ge(acc_done, (k + 1) * (KC - 1))
                for j in range(c0, c1):
                    last = nc.tensor.matmul(dst[:, j - c0:j - c0 + 1], acc[:, j * P:(j + 1) * P],
                                            ones[:, 0:1], start=True, stop=True)
                last.then_inc(colsum_done, 1)

            def spread(k, dst, c0, c1):
                pe.wait_ge(diag_done, k)
                for j in range(c0, c1):
                    b, o = divmod(j - c0, 4)
                    last = nc.tensor.matmul(dst[:, b, o * P:(o + 1) * P], ones[:], t_a[:, j * P:(j + 1) * P],
                                            start=True, stop=True)
                last.then_inc(bcast_done, 1)

            def first_two(norm, spread_k, u, q):
                project(u, u, q, 0, lambda k: pe.wait_ge(xs_ready, norm * KC + k + 1))
                column_sums(norm, pdn[:, 0, :], 0, KC)
                project(u + 1, u + 1, q + 1, 1,
                        lambda k: spread(spread_k, pdn[:, 1:3, :], 0, KC) if k == 4 else None)

            def ffn(layer, norm, spread_k, last_banks):
                U, Q, N, A = FFN_U[layer], FFN_Q[layer], FFN_N[layer], FFN_A[layer]
                first_two(norm, spread_k, U, Q)
                project(U + 2, U + 2, Q + 2, 0)
                project(U + 3, U + 3, Q + 3, 1)
                with pe.Fori(0, (FG - 1) // 2) as i:
                    for odd in (1, 2):
                        g = i * 2 + odd
                        for j in range(4):
                            project(ffn_in_unit(layer, g) + j, U - 2 + 6 * odd + j, g * 4 + (Q + j), j % 2)
                        down(ffn_down_unit(layer, g - 1), U + 2 + 6 * odd, i * 4 + (A + 2 * (odd - 1)),
                             i * 32 + (N + 16 * (odd - 1)), odd - 1)
                last = U + 3 * FC - 2
                last_banks(last, A + FC - 2, N + 16 * (FG - 1), FG - 1)

            pe.wait_ge(ones_set, 1)
            first_two(NORM_CONV, 1, CONV_U, CONV_Q)
            for g in range(CG):
                for j in range(6):
                    if g or j >= 2:
                        u, q = conv_in_unit(g) + j, 6 * g + j
                        project(u, u, q, q % 2)
                if g:
                    down(conv_down_unit(g - 1), conv_down_unit(g - 1), CONV_A + 2 * (g - 1), 16 * (g - 1), g - 1)
            down(conv_down_unit(CG - 1), conv_down_unit(CG - 1), CONV_A + KC - 2, 16 * (CG - 1), CG - 1)

            ffn(0, NORM_FFN0, 2, lambda u, a, base, odd: down(u, u, a, base, odd))

            def feature_transform(g):
                pe.wait_ge(xs_ready, NORM_FOUR * KC + g + 1)
                for c in range(KC):
                    if g and c == 0:
                        pe.wait_ge(z_lo, g)
                    if g and c == 4:
                        pe.wait_ge(z_hi, g)
                    rows = slice(c * P, (c + 1) * P)
                    for i, (st, mv) in enumerate(passes(xs_h[:, g, rows], xs_l[:, g, rows],
                                                        feat_h[:], feat_l[:])):
                        last = nc.tensor.matmul(pin[:, c // 2, (c % 2) * 256:(c % 2 + 1) * 256], st, mv,
                                                start=i == 0, stop=i == 2)
                        if g == 0 and c == 0 and i == 0:
                            last.then_inc(unit_used, 1)
                    if c % 4 == 3:
                        last.then_inc(z_done, 1)

            def position_transform(g):
                if g >= 2:
                    pe.wait_ge(y_made, g - 1)
                for fold in range(2):
                    pe.wait_ge(fold_ready, 2 * g + fold + 1)
                    mid = 2 * (g % 2) + fold
                    for wave in range(2):
                        t = 2 * fold + wave
                        table = (FOUR_U + t) % RING
                        out = pdn[:, 2 * (g % 2) + wave, fold * 256:(fold + 1) * 256]
                        for c in range(4):
                            if t == 1 and c == 1:
                                for b in range(4):
                                    cos = slice(b * 256, b * 256 + P)
                                    for z in (mid_h[:, mid, cos], mid_l[:, mid, cos]):
                                        nc.tensor.matmul(out[:, 0:2], z, alt[:], start=False, stop=False)
                            st = slice(c * 256 + wave * P, c * 256 + (wave + 1) * P)
                            mv = slice(c * 256, (c + 1) * 256)
                            for i, (z, w) in enumerate(passes(mid_h[:, mid, st], mid_l[:, mid, st],
                                                              ring_h[:, table, mv], ring_l[:, table, mv])):
                                last = nc.tensor.matmul(out, z, w, start=c == 0 and i == 0,
                                                        stop=c == 3 and i == 2)
                        if g == KC - 1 and t < 3:
                            last.then_inc(unit_used, 1)
                last.then_inc(y_done, 1)

            pe.wait_ge(feat_ready, 1)
            pe.wait_ge(alt_ready, 1)
            feature_transform(0)
            column_sums(NORM_FOUR, pdn[:, 0, :], 0, KC)
            pe.wait_ge(unit_ready, FOUR_U + 4)
            for g in range(KC):
                if g < KC - 1:
                    feature_transform(g + 1)
                position_transform(g)
            for m in range(KC):
                u = FOUR_U + 4 + m
                project(u, u, FOUR_Q + m, m % 2,
                        (lambda k: pe.wait_ge(y_ready, k + 1)) if m == 0 else None)

            def last_banks(u, a, base, odd):
                down(u, u, a, base, odd, range(0, 12), True)
                column_sums(NORM_FINAL, pin[:, 0, :], 0, 4)
                down(u, u, a, base, odd, range(12, 14), True)
                spread(4, pin[:, 1:2, :], 0, 4)
                down(u, u, a, base, odd, range(14, 16), True)
                column_sums(NORM_FINAL + 1, pin[:, 2, :], 4, 8)
                spread(5, pin[:, 3:4, :], 4, 8)

            ffn(1, NORM_FFN1, 3, last_banks)


def dft_tables():
    import numpy as np

    s = np.arange(S // 2)[:, None]
    j = np.arange(S // 4)[None, :]
    even = 2 * np.pi * ((s * 2 * j) % S) / S
    odd = 2 * np.pi * ((s * (2 * j + 1)) % S) / S
    waves = [np.cos(even), np.sin(even), np.cos(odd), np.sin(odd)]
    waves[1][:, 0] = 0.0
    seq = np.stack([w.reshape(4, P, S // 4).transpose(1, 0, 2).reshape(P, D) for w in waves]) * S ** -0.5
    d = np.arange(P)
    turn = 2 * np.pi * ((d[:, None] * d[None, :]) % P) / P
    feat = np.concatenate([np.cos(turn), np.sin(turn)], axis=1) * P ** -0.5
    cst = np.zeros((P, P + 2))
    cst[:, 0:P] = np.eye(P)
    cst[:, P] = (1.0 - 2.0 * (d % 2)) * S ** -0.5
    return [a.astype(np.float32) for a in (seq.reshape(4 * P, D), feat, cst)]


def kernel(x, conv_w_in, conv_k, conv_w_out, fourier_w_out, mix_norm_g, ffn_norm_g, ffn_w_gate, ffn_w_up,
           ffn_w_down, final_norm_g):
    import numpy as np
    import concourse.bacc as bacc
    from concourse.bass_utils import run_bass_kernel_spmd

    def column_units(w):
        w = np.asarray(w)
        n = w.shape[-1] // P
        w = w.reshape(-1, KC, P, n, P).transpose(0, 3, 2, 1, 4)
        return np.ascontiguousarray(w.reshape(-1, D))

    gains = [mix_norm_g[0], ffn_norm_g[0], mix_norm_g[1], ffn_norm_g[1], final_norm_g]
    gains = np.stack([np.asarray(g) for g in gains]).reshape(5, KC, P).transpose(2, 0, 1)
    taps = np.asarray(conv_k)[0].reshape(3, KC, P).transpose(2, 0, 1)
    seq, feat, cst = dft_tables()
    arrays = {
        "xT": np.ascontiguousarray(np.asarray(x)[0].T),
        "w_in": column_units(conv_w_in),
        "w_conv": np.ascontiguousarray(np.asarray(conv_w_out)[0]),
        "w_four": column_units(fourier_w_out),
        "w_gate": column_units(ffn_w_gate),
        "w_up": column_units(ffn_w_up),
        "w_down": np.ascontiguousarray(np.asarray(ffn_w_down).reshape(2 * FF, D)),
        "gains": np.ascontiguousarray(gains),
        "taps": np.ascontiguousarray(taps),
        "seq": seq,
        "feat": feat,
        "cst": cst,
    }
    nc = bacc.Bacc("TRN2", target_bir_lowering=False, num_devices=1)
    args = [nc.dram_tensor(name + "_dram", a.shape, mybir.dt.float32, kind="ExternalInput").ap()
            for name, a in arrays.items()]
    out = nc.dram_tensor("out_dram", (D, S), mybir.dt.float32, kind="ExternalOutput").ap()
    build(nc, *args, out)
    result = run_bass_kernel_spmd(nc, [{name + "_dram": a for name, a in arrays.items()}], core_ids=[0])
    return np.ascontiguousarray(result.results[0]["out_dram"].T).reshape(1, S, D)
```

```python
import concourse.bass as bass
from concourse import mybir
from contextlib import ExitStack

P = 128
D = 1024
S = 1024
KC = D // P
HALF = 512
FF = 2816
FC = FF // P
FG = FC // 2
CG = KC // 2
RMS_EPS = 1e-5
RAW = 3
RING = 6
ACTS = 4
BANKS = 4
BY_START = 2
FINAL_DVE = 6
UNITS_IN_PAIR = 12

CONV_U = 0
FFN_U = [CONV_U + 4 * KC, 0]
FOUR_U = FFN_U[0] + 3 * FC
FFN_U[1] = FOUR_U + 4 + KC
CONV_Q = 0
FFN_Q = [3 * KC, 3 * KC + 2 * FC + KC]
FOUR_Q = FFN_Q[0] + 2 * FC
CONV_N = 0
FFN_N = [16 * CG, 16 * (CG + FG)]
CONV_A = 0
FFN_A = [KC, KC + FC]
NORM_CONV, NORM_FFN0, NORM_FOUR, NORM_FFN1, NORM_FINAL = range(5)
ADDS = [KC - 1, KC - 1, KC - 2, KC - 1, KC - 2, KC - 2]


def adds_before(norm):
    return sum(ADDS[:norm])


def conv_in_unit(g):
    return CONV_U + (0 if g == 0 else 8 * g - 2)


def conv_down_unit(g):
    return CONV_U + (8 * g + 12 if g < CG - 1 else 4 * KC - 2)


def ffn_in_unit(layer, g):
    return g * 6 + (FFN_U[layer] - 2)


def ffn_down_unit(layer, g):
    return g * 6 + (FFN_U[layer] + 8)


def start_steps():
    steps = [(0, 0)]
    for k in range(1, KC):
        steps += [(0, k), (1, k - 1)]
    return steps + [(1, KC - 1)]


def build(nc, xT, w_in, w_conv, w_four, w_gate, w_up, w_down, gains_d, taps_d, seq_d, feat_d, cst_d, outT):
    F32 = mybir.dt.float32
    F32R = mybir.dt.float32r
    ALU = mybir.AluOpType
    ACT = mybir.ActivationFunctionType

    ctx = ExitStack()
    with ctx:
        def sb(name, shape, dt=F32):
            return ctx.enter_context(nc.sbuf_tensor(name, shape, dt))

        def sem(name):
            return ctx.enter_context(nc.semaphore(name))

        res = sb("res", [P, KC, S])
        xs_h = sb("xs_h", [P, KC, S], F32R)
        xs_l = sb("xs_l", [P, KC, S], F32R)
        mid_h = sb("mid_h", [P, ACTS, S], F32R)
        mid_l = sb("mid_l", [P, ACTS, S], F32R)
        raw = sb("raw", [P, RAW, D])
        ring_h = sb("ring_h", [P, RING, D], F32R)
        ring_l = sb("ring_l", [P, RING, D], F32R)
        t_a = sb("t_a", [P, S])
        t_b = sb("t_b", [P, S])
        padded = sb("padded", [P, S + 2])
        acc = padded[:, 1:S + 1]
        rb = sb("rb", [P, S])
        gains = sb("gains", [P, 5, KC])
        taps = sb("taps", [P, 3, KC])
        cst = sb("cst", [P, P + 2])
        ident = cst[:, 0:P]
        ones = sb("ones", [P, P])
        feat_h = sb("feat_h", [P, 2 * P], F32R)
        feat_l = sb("feat_l", [P, 2 * P], F32R)
        alt = sb("alt", [P, 2], F32R)
        stat = sb("stat", [P, KC])
        root = sb("root", [P, KC])
        step = sb("step", [P, KC])
        rcol = sb("rcol", [P, KC])

        pin = ctx.enter_context(nc.psum_tensor("pin", [P, 4, HALF], F32))
        pdn = ctx.enter_context(nc.psum_tensor("pdn", [P, BANKS, HALF], F32))

        def in_pair(q):
            return pdn[:, 2:4, :] if q == 2 else pin[:, 2 * (q % 2):2 * (q % 2) + 2, :]

        raw_landed = [sem(f"raw_landed{i}") for i in range(RAW)]
        start_landed = [sem(f"start_landed{i}") for i in range(BY_START)]
        start_high = sem("start_high")
        start_ready = sem("start_ready")
        unit_high = sem("unit_high")
        unit_ready = sem("unit_ready")
        unit_used = sem("unit_used")
        x_landed = [sem(f"x_landed{i}") for i in range(KC)]
        gains_landed = sem("gains_landed")
        small_landed = sem("small_landed")
        feat_landed = sem("feat_landed")
        feat_high = sem("feat_high")
        feat_ready = sem("feat_ready")
        ones_set = sem("ones_set")
        alt_ready = sem("alt_ready")
        edges_set = sem("edges_set")
        xs_high = sem("xs_high")
        xs_ready = sem("xs_ready")
        sq_done = sem("sq_done")
        acc_done = sem("acc_done")
        colsum_done = sem("colsum_done")
        stat_done = sem("stat_done")
        root_done = sem("root_done")
        newton = sem("newton")
        rcol_ready = sem("rcol_ready")
        diag_done = sem("diag_done")
        bcast_done = sem("bcast_done")
        rb_ready = sem("rb_ready")
        in_done = sem("in_done")
        in_free = sem("in_free")
        gate2 = sem("gate2")
        tap_mid = sem("tap_mid")
        tap_left = sem("tap_left")
        tap_right = sem("tap_right")
        silu_done = sem("silu_done")
        mid_made = sem("mid_made")
        mid_high = sem("mid_high")
        mid_ready = sem("mid_ready")
        down_done = sem("down_done")
        down_added = sem("down_added")
        z_done = sem("z_done")
        z_lo = sem("z_lo")
        z_hi = sem("z_hi")
        plus_made = sem("plus_made")
        minus_made = sem("minus_made")
        plus_high = sem("plus_high")
        minus_high = sem("minus_high")
        fold_ready = sem("fold_ready")
        y_done = sem("y_done")
        y_cos = sem("y_cos")
        y_made = sem("y_made")
        y_high = sem("y_high")
        y_ready = sem("y_ready")
        y_spent = sem("y_spent")
        gained = sem("gained")
        scaled = [sem("scaled_dve"), sem("scaled_pool")]
        stored = sem("stored")

        block = ctx.enter_context(nc.Block())

        @block.sync
        def _(sp):
            def load_unit(u, slot_of, src):
                if isinstance(u, int) and u - RAW < BY_START:
                    if u >= RAW:
                        sp.wait_ge(start_ready, 2 + u - RAW + 1)
                else:
                    sp.wait_ge(unit_ready, u - (RAW - 1 + BY_START))
                sp.dma_start(raw[:, slot_of % RAW, :], src).then_inc(raw_landed[slot_of % RAW], 16)

            def col_rows(w, f):
                return w[bass.ds(f * P, P), :]

            def conv_in(g):
                u = conv_in_unit(g)
                for j in range(2):
                    for part in (1, 2, 0):
                        load_unit(u, u, col_rows(w_in, part * KC + 2 * g + j))
                        u += 1

            def conv_down(g):
                for j in range(2):
                    u = conv_down_unit(g) + j
                    load_unit(u, u, col_rows(w_conv, 2 * g + j))

            def ffn_in(layer, g, u, slot):
                for j in range(2):
                    for w in (w_gate, w_up):
                        load_unit(u, slot, col_rows(w, g * 2 + (layer * FC + j)))
                        u, slot = u + 1, slot + 1

            def ffn_down(layer, g, u, slot):
                for j in range(2):
                    load_unit(u + j, slot + j, col_rows(w_down, g * 2 + (layer * FC + j)))

            def ffn(layer):
                ffn_in(layer, 0, FFN_U[layer], FFN_U[layer])
                with sp.Fori(0, (FG - 1) // 2) as i:
                    for odd in (1, 2):
                        g = i * 2 + odd
                        ffn_in(layer, g, ffn_in_unit(layer, g), FFN_U[layer] - 2 + 6 * odd)
                        ffn_down(layer, g - 1, ffn_down_unit(layer, g - 1), FFN_U[layer] + 2 + 6 * odd)
                last = FFN_U[layer] + 3 * FC - 2
                ffn_down(layer, FG - 1, last, last)

            def load_x(first, end):
                for m in range(first, end):
                    sp.dma_start(res[:, m, :], xT[m * P:(m + 1) * P, :]).then_inc(x_landed[m], 16)

            def load_start(half):
                cols = slice(half * D // 2, (half + 1) * D // 2)
                for u in range(BY_START):
                    landed = raw_landed[u] if half else start_landed[u]
                    sp.dma_start(raw[:, u, cols], col_rows(w_in, (u + 1) * KC)[:, cols]).then_inc(landed, 16)

            load_x(0, 1)
            load_start(0)
            load_x(1, 3)
            load_start(1)
            load_x(3, KC)
            for g in range(CG):
                if g == 0:
                    rest = [(0, 0), (1, 1), (1, 2), (1, 0)]
                    for n, (j, part) in enumerate(rest):
                        load_unit(BY_START + n, BY_START + n, col_rows(w_in, part * KC + j))
                else:
                    conv_in(g)
                    conv_down(g - 1)
            conv_down(CG - 1)
            ffn(0)
            for t in range(4):
                load_unit(FOUR_U + t, FOUR_U + t, seq_d[t * P:(t + 1) * P, :])
            for m in range(KC):
                load_unit(FOUR_U + 4 + m, FOUR_U + 4 + m, col_rows(w_four, m))
            ffn(1)
            for h in range(2):
                for m in range(KC):
                    if m < FINAL_DVE:
                        sp.wait_ge(scaled[0], h * FINAL_DVE + m + 1)
                    else:
                        sp.wait_ge(scaled[1], (h - 1) * (KC - FINAL_DVE) + m + 1 - FINAL_DVE + KC - FINAL_DVE)
                    sp.dma_start(outT[m * P:(m + 1) * P, h * HALF:(h + 1) * HALF],
                                 res[:, m, h * HALF:(h + 1) * HALF]).then_inc(stored, 16)
            sp.wait_ge(stored, 16 * 2 * KC)

        @block.gpsimd
        def _(pool):
            def split_unit(u, slot_of, landed):
                pool.wait_ge(raw_landed[slot_of % RAW], landed * 16)
                if not isinstance(u, int) or u >= RING:
                    pool.wait_ge(unit_used, u - (RING - 1))
                src = raw[:, slot_of % RAW, :]
                high = ring_h[:, slot_of % RING, :]
                blocks = [ap.rearrange("p (c n) -> p c n", n=P) for ap in (high, src)]
                one = ones[:].rearrange("p (c n) -> p c n", c=1).to_broadcast([P, KC, P])
                nc.gpsimd.tensor_tensor(blocks[0], blocks[1], one, ALU.mult).then_inc(unit_high, 1)
                pool.wait_ge(unit_high, u + (1 - BY_START))
                nc.gpsimd.tensor_tensor(ring_l[:, slot_of % RING, :], src, high.bitcast(F32),
                                        ALU.subtract).then_inc(unit_ready, 1)

            def split_units(first, end):
                for u in range(first, end):
                    split_unit(u, u, u // RAW + 1)

            def add_square(norm, m):
                pool.wait_ge(sq_done, norm * KC + m + 1)
                if m >= 2:
                    pool.wait_ge(acc_done, adds_before(norm) + m - 1)
                sq = t_a if m % 2 else t_b
                nc.gpsimd.tensor_tensor(acc, acc, sq[:], ALU.add).then_inc(acc_done, 1)

            def ffn(layer):
                first = FFN_U[layer] + 4
                with pool.Fori(0, (FG - 1) // 2) as i:
                    for j in range(UNITS_IN_PAIR):
                        u = first + j
                        split_unit(i * UNITS_IN_PAIR + u, u, i * (UNITS_IN_PAIR // RAW) + (u // RAW + 1))
                split_units(FFN_U[layer] + 3 * FC - 2, FFN_U[layer] + 3 * FC)

            nc.gpsimd.memset(ones[:], 1.0).then_inc(ones_set, 1)
            nc.gpsimd.memset(padded[:, 0:1], 0.0).then_inc(edges_set, 1)
            nc.gpsimd.memset(padded[:, S + 1:S + 2], 0.0).then_inc(edges_set, 1)
            pool.wait_ge(ones_set, 1)
            for m in range(1, KC):
                add_square(NORM_CONV, m)
                if m == 6:
                    split_units(BY_START, BY_START + 1)
            pool.wait_ge(feat_landed, 16)
            nc.gpsimd.tensor_copy(feat_h[:], rb[:, 0:2 * P]).then_inc(feat_high, 1)
            pool.wait_ge(feat_high, 1)
            nc.gpsimd.tensor_tensor(feat_l[:], rb[:, 0:2 * P], feat_h[:].bitcast(F32),
                                    ALU.subtract).then_inc(feat_ready, 1)
            split_units(BY_START + 1, FFN_U[0] + 4)
            for m in range(1, KC):
                add_square(NORM_FFN0, m)
            ffn(0)
            split_units(FOUR_U, FOUR_U + 4)
            for m in range(1, KC - 1):
                add_square(NORM_FOUR, m)
            split_units(FOUR_U + 4, FOUR_U + 6)
            for g in range(KC):
                pool.wait_ge(y_high, g + 1)
                nc.gpsimd.tensor_tensor(xs_l[:, g, :], rb[:], xs_h[:, g, :].bitcast(F32),
                                        ALU.subtract).then_inc(y_ready, 1)
            split_units(FOUR_U + 6, FOUR_U + 10)
            for m in range(KC):
                if m:
                    add_square(NORM_FFN1, m)
                if m < 6:
                    split_units(FOUR_U + 10 + m, FOUR_U + 11 + m)
            ffn(1)
            for h in range(2):
                cols = slice(h * HALF, (h + 1) * HALF)
                for m in range(1, KC - 1):
                    pool.wait_ge(sq_done, (NORM_FINAL + h) * KC + m + 1)
                    if m >= 2:
                        pool.wait_ge(acc_done, adds_before(NORM_FINAL + h) + m - 1)
                    sq = t_a if m % 2 else t_b
                    nc.gpsimd.tensor_tensor(acc[:, cols], acc[:, cols], sq[:, cols],
                                            ALU.add).then_inc(acc_done, 1)
            for h in range(2):
                cols = slice(h * HALF, (h + 1) * HALF)
                pool.wait_ge(rb_ready, 4 + h)
                for m in range(FINAL_DVE, KC):
                    pool.wait_ge(gained, KC * h + m + 1)
                    nc.gpsimd.tensor_tensor(res[:, m, cols], res[:, m, cols], rb[:, cols],
                                            ALU.mult).then_inc(scaled[1], 1)

        @block.scalar
        def _(act):
            def norm_high(norm, m):
                nc.scalar.activation(xs_h[:, m, :], res[:, m, :], ACT.Copy,
                                     scale=gains[:, norm, m:m + 1]).then_inc(xs_high, 1)

            def norm_square(norm, m):
                if m >= 3:
                    act.wait_ge(acc_done, adds_before(norm) + m - 2)
                sq = acc if m == 0 else t_a[:] if m % 2 else t_b[:]
                nc.scalar.activation(sq, res[:, m, :], ACT.Square).then_inc(sq_done, 1)

            def norm_feed(norm, wait_chunk):
                nc.scalar.preload_act_table(ACT.Sqrt)
                for m in range(KC):
                    wait_chunk(m)
                    norm_square(norm, m)
                    norm_high(norm, m)

            def norm_root(k, c0, c1):
                act.wait_ge(stat_done, k + 1)
                nc.scalar.activation(root[:, c0:c1], stat[:, c0:c1], ACT.Sqrt).then_inc(root_done, 1)

            def norm_spread(k, c0, c1):
                act.wait_ge(bcast_done, k)
                n = (c1 - c0) // HALF
                nc.scalar.activation(rb[:, c0:c1], pdn[:, 0:n, :], ACT.Copy).then_inc(rb_ready, 1)

            def mid_round(a, slot):
                act.wait_ge(mid_made, a + 1)
                nc.scalar.activation(mid_h[:, slot, :], t_b[:], ACT.Copy).then_inc(mid_high, 1)

            def conv_chunk(f):
                act.wait_ge(in_free, 3 * f + 2)
                nc.scalar.activation(t_a[:], acc, ACT.Copy, scale=taps[:, 1, f:f + 1]).then_inc(tap_mid, 1)
                mid_round(f, f % ACTS)

            def ffn_group(layer, g, odd):
                for j in range(2):
                    act.wait_ge(in_free, g * 4 + (FFN_Q[layer] + 2 * j + 1))
                    nc.scalar.activation(t_a[:], t_a[:], ACT.Silu).then_inc(silu_done, 1)
                    mid_round(g * 2 + (FFN_A[layer] + j), 2 * (odd % 2) + j)

            def ffn(layer):
                ffn_group(layer, 0, 0)
                with act.Fori(0, (FG - 1) // 2) as i:
                    for odd in (1, 2):
                        ffn_group(layer, i * 2 + odd, odd)

            def last_down(base, norm):
                def wait_chunk(m):
                    act.wait_ge(down_added, base + 2 * m + 2)
                norm_feed(norm, wait_chunk)

            nc.scalar.preload_act_table(ACT.Sqrt)
            act.dma_start(gains[:], gains_d).then_inc(gains_landed, 16)
            act.dma_start(taps[:], taps_d).then_inc(small_landed, 16)
            act.dma_start(cst[:], cst_d).then_inc(small_landed, 16)
            act.dma_start(rb[:, 0:2 * P], feat_d).then_inc(feat_landed, 16)
            act.wait_ge(gains_landed, 16)

            def start_unit_high(u, half):
                act.wait_ge(raw_landed[u] if half else start_landed[u], 16)
                cols = slice(half * D // 2, (half + 1) * D // 2)
                nc.scalar.activation(ring_h[:, u, cols], raw[:, u, cols], ACT.Copy).then_inc(start_high, 1)

            for m in range(KC):
                act.wait_ge(x_landed[m], 16)
                norm_high(NORM_CONV, m)
                if m in (0, 2):
                    for u in range(BY_START):
                        start_unit_high(u, m // 2)
                norm_square(NORM_CONV, m)
            act.wait_ge(small_landed, 16 * 2)
            nc.scalar.activation(alt[:], cst[:, P:P + 2], ACT.Copy).then_inc(alt_ready, 1)
            norm_root(NORM_CONV, 0, KC)
            act.wait_ge(feat_ready, 1)
            norm_spread(NORM_CONV + 1, 0, S)
            for f in range(KC):
                conv_chunk(f)
            act.wait_ge(mid_ready, CONV_A + KC)
            last_down(CONV_N + 16 * (CG - 1), NORM_FFN0)
            norm_root(NORM_FFN0, 0, KC)
            norm_spread(NORM_FFN0 + 1, 0, S)
            ffn(0)
            act.wait_ge(mid_ready, FFN_A[0] + FC)
            last_down(FFN_N[0] + 16 * (FG - 1), NORM_FOUR)
            norm_root(NORM_FOUR, 0, KC)
            act.wait_ge(rcol_ready, NORM_FOUR + 1)

            def y_leaves(g):
                act.wait_ge(y_done, g + 1)
                if g:
                    act.wait_ge(y_ready, g)
                nc.scalar.activation(rb[:, 0:HALF].rearrange("p (j e) -> p j e", e=2),
                                     pdn[:, 2 * (g % 2), :].rearrange("p (e j) -> p j e", e=2),
                                     ACT.Copy).then_inc(y_cos, 1)
                act.wait_ge(y_made, g + 1)
                nc.scalar.activation(xs_h[:, g, :], rb[:], ACT.Copy).then_inc(y_high, 1)

            for g in range(KC):
                act.wait_ge(z_done, 2 * g + 1)
                if g:
                    act.wait_ge(fold_ready, 2 * g)
                for c in range(4):
                    last = nc.scalar.activation(t_a[:, c * 256:(c + 1) * 256],
                                                pin[:, c // 2, (c % 2) * 256:(c % 2 + 1) * 256],
                                                ACT.Copy, scale=rcol[:, c:c + 1])
                last.then_inc(z_lo, 1)
                act.wait_ge(plus_made, g + 1)
                nc.scalar.activation(mid_h[:, 2 * (g % 2), :], acc, ACT.Copy).then_inc(plus_high, 1)
                act.wait_ge(minus_made, g + 1)
                nc.scalar.activation(mid_h[:, 2 * (g % 2) + 1, :], t_a[:], ACT.Copy).then_inc(minus_high, 1)
                if g:
                    y_leaves(g - 1)
            y_leaves(KC - 1)

            for m in range(KC):
                act.wait_ge(in_free, FOUR_Q + m + 1)
                norm_square(NORM_FFN1, m)
                if m == KC - 2:
                    for k in range(KC - 1):
                        act.wait_ge(y_spent, k + 1)
                        norm_high(NORM_FFN1, k)
            act.wait_ge(in_done, FOUR_Q + KC)
            norm_high(NORM_FFN1, KC - 1)
            norm_root(NORM_FFN1, 0, KC)
            norm_spread(NORM_FFN1, 0, S)
            ffn(1)
            def final_squares(h, first, end):
                cols = slice(h * HALF, (h + 1) * HALF)
                for m in range(first, end):
                    act.wait_ge(down_added, FFN_N[1] + 16 * (FG - 1) + KC * h + m + 1)
                    if m >= 3:
                        act.wait_ge(acc_done, adds_before(NORM_FINAL + h) + m - 2)
                    sq = acc if m == 0 else t_a if m % 2 else t_b
                    nc.scalar.activation(sq[:, cols], res[:, m, cols], ACT.Square).then_inc(sq_done, 1)

            def final_spread(h):
                act.wait_ge(bcast_done, NORM_FINAL + h)
                nc.scalar.activation(rb[:, h * HALF:(h + 1) * HALF], pin[:, 2 * h + 1, :],
                                     ACT.Copy).then_inc(rb_ready, 1)

            act.wait_ge(mid_ready, FFN_A[1] + FC)
            nc.scalar.preload_act_table(ACT.Sqrt)
            final_squares(0, 0, KC)
            final_squares(1, 0, 4)
            norm_root(NORM_FINAL, 0, 4)
            final_squares(1, 4, 6)
            final_spread(0)
            final_squares(1, 6, KC)
            norm_root(NORM_FINAL + 1, 4, 8)
            final_spread(1)

        @block.vector
        def _(dve):
            def norm_low(norm, m):
                dve.wait_ge(xs_high, norm * KC + m + 1)
                nc.vector.scalar_tensor_tensor(xs_l[:, m, :], res[:, m, :], gains[:, norm, m:m + 1],
                                               xs_h[:, m, :].bitcast(F32), ALU.mult,
                                               ALU.subtract).then_inc(xs_ready, 1)

            def norm_column(k, colsum, c0, c1):
                dve.wait_ge(colsum_done, k + 1)
                nc.vector.tensor_scalar(stat[:, c0:c1], colsum, 1.0 / D, RMS_EPS, ALU.mult,
                                        ALU.add).then_inc(stat_done, 1)
                dve.wait_ge(root_done, k + 1)
                nc.vector.reciprocal(rcol[:, c0:c1], root[:, c0:c1]).then_inc(newton, 1)
                dve.wait_ge(newton, 4 * k + 1)
                nc.vector.tensor_tensor(step[:, c0:c1], rcol[:, c0:c1], rcol[:, c0:c1], ALU.mult).then_inc(newton, 1)
                dve.wait_ge(newton, 4 * k + 2)
                nc.vector.tensor_tensor(step[:, c0:c1], step[:, c0:c1], stat[:, c0:c1], ALU.mult).then_inc(newton, 1)
                dve.wait_ge(newton, 4 * k + 3)
                nc.vector.tensor_scalar(step[:, c0:c1], step[:, c0:c1], -0.5, 1.5, ALU.mult, ALU.add).then_inc(newton, 1)
                dve.wait_ge(newton, 4 * k + 4)
                nc.vector.tensor_tensor(rcol[:, c0:c1], rcol[:, c0:c1], step[:, c0:c1], ALU.mult).then_inc(rcol_ready, 1)
                dve.wait_ge(rcol_ready, k + 1)

            def norm_diag(c0, c1):
                n = c1 - c0
                nc.vector.tensor_tensor(
                    t_a[:, c0 * P:c1 * P].rearrange("p (j n) -> p j n", n=P),
                    ident.rearrange("p (j n) -> p j n", j=1).to_broadcast([P, n, P]),
                    rcol[:, c0:c1].rearrange("p (j n) -> p j n", n=1).to_broadcast([P, n, P]),
                    ALU.mult).then_inc(diag_done, 1)

            def scale_out(q, pair, dst):
                dve.wait_ge(in_done, q + 1)
                nc.vector.tensor_tensor(dst, pair.rearrange("p b n -> p (b n)"), rb[:],
                                        ALU.mult).then_inc(in_free, 1)
                dve.wait_ge(in_free, q + 1)

            def mid_low(a, slot):
                dve.wait_ge(mid_high, a + 1)
                nc.vector.tensor_tensor(mid_l[:, slot, :], t_b[:], mid_h[:, slot, :].bitcast(F32),
                                        ALU.subtract).then_inc(mid_ready, 1)

            def down_add(n, m, h, bank):
                dve.wait_ge(down_done, n + 1)
                cols = slice(h * HALF, (h + 1) * HALF)
                nc.vector.tensor_tensor(res[:, m, cols], pdn[:, bank, :], res[:, m, cols],
                                        ALU.add).then_inc(down_added, 1)

            def down_adds(base, first, end):
                for n in range(first, end):
                    down_add(base + n, n // 2, n % 2, n % BANKS)

            def last_down(base, norm):
                for m in range(KC):
                    down_adds(base, 2 * m, 2 * m + 2)
                    if m:
                        norm_low(norm, m - 1)
                norm_low(norm, KC - 1)

            def conv_chunk(f, tail):
                q = 3 * f
                scale_out(q, in_pair(q), t_a[:])
                nc.vector.tensor_tensor(t_a[:], t_a[:], rb[:], ALU.mult).then_inc(gate2, 1)
                dve.wait_ge(gate2, f + 1)
                dve.wait_ge(in_done, q + 2)
                nc.vector.tensor_tensor(acc, in_pair(q + 1).rearrange("p b n -> p (b n)"),
                                        t_a[:], ALU.mult).then_inc(in_free, 1)
                dve.wait_ge(in_free, q + 2)
                dve.wait_ge(tap_mid, f + 1)
                nc.vector.scalar_tensor_tensor(t_a[:], padded[:, 0:S], taps[:, 0, f:f + 1], t_a[:],
                                               ALU.mult, ALU.add).then_inc(tap_left, 1)
                dve.wait_ge(tap_left, f + 1)
                nc.vector.scalar_tensor_tensor(t_a[:], padded[:, 2:S + 2], taps[:, 2, f:f + 1], t_a[:],
                                               ALU.mult, ALU.add).then_inc(tap_right, 1)
                dve.wait_ge(tap_right, f + 1)
                scale_out(q + 2, in_pair(q + 2), t_b[:])
                nc.vector.tensor_tensor(t_b[:], t_b[:], t_a[:], ALU.mult).then_inc(mid_made, 1)
                tail()
                mid_low(f, f % ACTS)

            def ffn_group(layer, g, odd, down_base):
                for j in range(2):
                    q = g * 4 + (FFN_Q[layer] + 2 * j)
                    a = g * 2 + (FFN_A[layer] + j)
                    scale_out(q, pin[:, 0:2, :], t_a[:])
                    scale_out(q + 1, pin[:, 2:4, :], t_b[:])
                    dve.wait_ge(silu_done, a - (KC - 1))
                    nc.vector.tensor_tensor(t_b[:], t_b[:], t_a[:], ALU.mult).then_inc(mid_made, 1)
                    if j and down_base is not None:
                        down_adds(down_base, 0, 2)
                    mid_low(a, 2 * (odd % 2) + j)
                if down_base is not None:
                    down_adds(down_base, 2, 16)

            def ffn(layer):
                ffn_group(layer, 0, 0, None)
                with dve.Fori(0, (FG - 1) // 2) as i:
                    for odd in (1, 2):
                        g = i * 2 + odd
                        ffn_group(layer, g, odd, i * 32 + (FFN_N[layer] + 16 * (odd - 1)))

            dve.wait_ge(gains_landed, 16)
            dve.wait_ge(edges_set, 2)
            def start_unit_low(u, n, half):
                dve.wait_ge(start_high, n)
                cols = slice(half * D // 2, (half + 1) * D // 2)
                nc.vector.tensor_tensor(ring_l[:, u, cols], raw[:, u, cols], ring_h[:, u, cols].bitcast(F32),
                                        ALU.subtract).then_inc(start_ready, 1)

            for m in range(KC):
                norm_low(NORM_CONV, m)
                if m in (0, 2):
                    for u in range(BY_START):
                        start_unit_low(u, m + u + 1, m // 2)
            dve.wait_ge(small_landed, 16 * 2)
            norm_column(NORM_CONV, pdn[:, 0, 0:KC], 0, KC)
            norm_diag(0, KC)
            dve.wait_ge(rb_ready, 1)
            for f in range(KC):
                g, j = divmod(f, 2)
                adds = j == 1 and g >= 1
                conv_chunk(f, (lambda: down_adds(16 * (g - 1), 0, 2)) if adds else (lambda: None))
                if adds:
                    down_adds(16 * (g - 1), 2, 16)
            last_down(CONV_N + 16 * (CG - 1), NORM_FFN0)
            norm_column(NORM_FFN0, pdn[:, 0, 0:KC], 0, KC)
            norm_diag(0, KC)
            dve.wait_ge(rb_ready, 2)
            ffn(0)
            last_down(FFN_N[0] + 16 * (FG - 1), NORM_FOUR)
            norm_column(NORM_FOUR, pdn[:, 0, 0:KC], 0, KC)

            def y_leaves(g):
                sine = pdn[:, 2 * (g % 2) + 1, :]
                y_even = rb[:].rearrange("p (j e) -> p j e", e=2)[:, :, 0]
                y_odd = rb[:].rearrange("p (j e) -> p j e", e=2)[:, :, 1]
                Q = S // 4
                dve.wait_ge(y_cos, g + 1)
                nc.vector.tensor_tensor(y_even[:, S // 2 - 1:Q:-1], y_even[:, 1:Q], sine[:, 1:Q], ALU.add)
                nc.vector.tensor_tensor(y_odd[:, S // 2 - 1:Q - 1:-1], y_odd[:, 0:Q], sine[:, Q:2 * Q], ALU.add)
                nc.vector.tensor_tensor(y_even[:, 1:Q], y_even[:, 1:Q], sine[:, 1:Q], ALU.subtract)
                nc.vector.tensor_tensor(y_odd[:, 0:Q], y_odd[:, 0:Q], sine[:, Q:2 * Q], ALU.subtract)
                nc.vector.tensor_copy(rb[:, S // 2:S // 2 + 1], sine[:, 0:1]).then_inc(y_made, 1)

            for g in range(KC):
                dve.wait_ge(z_done, 2 * g + 2)
                nc.vector.tensor_tensor(
                    t_b[:].rearrange("p (c n) -> p c n", c=4),
                    pin[:, 2:4, :].rearrange("p b (c n) -> p (b c) n", c=2),
                    rcol[:, 4:8].rearrange("p (c n) -> p c n", n=1).to_broadcast([P, 4, 256]),
                    ALU.mult).then_inc(z_hi, 1)
                dve.wait_ge(z_hi, g + 1)
                dve.wait_ge(z_lo, g + 1)
                nc.vector.tensor_tensor(acc, t_a[:], t_b[:], ALU.add).then_inc(plus_made, 1)
                nc.vector.tensor_tensor(t_a[:], t_a[:], t_b[:], ALU.subtract).then_inc(minus_made, 1)
                dve.wait_ge(plus_made, g + 1)
                dve.wait_ge(plus_high, g + 1)
                slot = 2 * (g % 2)
                nc.vector.tensor_tensor(mid_l[:, slot, :], acc, mid_h[:, slot, :].bitcast(F32),
                                        ALU.subtract).then_inc(fold_ready, 1)
                dve.wait_ge(minus_made, g + 1)
                dve.wait_ge(minus_high, g + 1)
                nc.vector.tensor_tensor(mid_l[:, slot + 1, :], t_a[:], mid_h[:, slot + 1, :].bitcast(F32),
                                        ALU.subtract).then_inc(fold_ready, 1)
                if g:
                    y_leaves(g - 1)
            y_leaves(KC - 1)
            for m in range(KC):
                q = FOUR_Q + m
                if m == KC - 1:
                    for k in range(KC - 1):
                        norm_low(NORM_FFN1, k)
                dve.wait_ge(in_done, q + 1)
                nc.vector.tensor_tensor(res[:, m, :], in_pair(q).rearrange("p b n -> p (b n)"),
                                        res[:, m, :], ALU.add).then_inc(in_free, 1)
            norm_low(NORM_FFN1, KC - 1)
            norm_column(NORM_FFN1, pdn[:, 0, 0:KC], 0, KC)
            norm_diag(0, KC)
            dve.wait_ge(rb_ready, 3)
            ffn(1)
            def final_gain(n):
                h, m = divmod(n, KC)
                cols = slice(h * HALF, (h + 1) * HALF)
                dve.wait_ge(sq_done, NORM_FINAL * KC + n + 1)
                nc.vector.tensor_scalar(res[:, m, cols], res[:, m, cols], gains[:, NORM_FINAL, m:m + 1],
                                        None, ALU.mult).then_inc(gained, 1)

            def final_adds(first, end):
                for n in range(first, end):
                    down_add(FFN_N[1] + 16 * (FG - 1) + n, n % KC, n // KC, n % BANKS)
                    if n:
                        final_gain(n - 1)

            def final_scale(h, first, end, r):
                cols = slice(h * HALF, (h + 1) * HALF)
                for m in range(first, end):
                    dve.wait_ge(gained, KC * h + m + 1)
                    nc.vector.tensor_tensor(res[:, m, cols], r, res[:, m, cols],
                                            ALU.mult).then_inc(scaled[0], 1)

            final_adds(0, 12)
            norm_column(NORM_FINAL, pin[:, 0, 0:4], 0, 4)
            norm_diag(0, 4)
            final_adds(12, 16)
            final_gain(15)
            dve.wait_ge(rb_ready, 4)
            final_scale(0, 0, 3, rb[:, 0:HALF])
            norm_column(NORM_FINAL + 1, pin[:, 2, 0:4], 4, 8)
            norm_diag(4, 8)
            final_scale(0, 3, FINAL_DVE, rb[:, 0:HALF])
            dve.wait_ge(rb_ready, 5)
            final_scale(1, 0, FINAL_DVE, rb[:, HALF:S])

        @block.tensor
        def _(pe):

            def passes(w_h, w_l, x_h, x_l):
                return ((w_h, x_h), (w_l, x_h), (w_h, x_l))

            def project_chunk(slot, pair, k, frees, signal=None):
                w = slice(k * P, (k + 1) * P)
                for h in range(2):
                    cols = slice(h * HALF, (h + 1) * HALF)
                    for i, (st, mv) in enumerate(passes(ring_h[:, slot, w], ring_l[:, slot, w],
                                                        xs_h[:, k, cols], xs_l[:, k, cols])):
                        last = nc.tensor.matmul(pair[:, h, :], st, mv,
                                                start=k == 0 and i == 0, stop=k == KC - 1 and i == 2)
                        if frees and h == 0 and i == 0:
                            last.then_inc(unit_used, 1)
                if signal is not None:
                    last.then_inc(signal, 1)

            def project(u, slot_of, q, pair, before_chunk=None, spent=None):
                pe.wait_ge(unit_ready, u + (1 - BY_START))
                if not isinstance(q, int) or q > 2:
                    pe.wait_ge(in_free, q - 1)
                for k in range(KC):
                    if before_chunk is not None:
                        before_chunk(k)
                    project_chunk(slot_of % RING, pair, k, k == 0, in_done if k == KC - 1 else spent)

            def down(u, slot_of, a, base, odd, banks=range(16), halves_outer=False):
                if banks[0] == 0:
                    pe.wait_ge(unit_ready, u + (2 - BY_START))
                    pe.wait_ge(mid_ready, a + 2)
                for n in banks:
                    h, m = divmod(n, KC) if halves_outer else (n % 2, n // 2)
                    if not isinstance(base, int) or base + n >= BANKS:
                        pe.wait_ge(down_added, base + (n - (BANKS - 1)))
                    w, cols = slice(m * P, (m + 1) * P), slice(h * HALF, (h + 1) * HALF)
                    for j in range(2):
                        slot, mid = (slot_of + j) % RING, 2 * (odd % 2) + j
                        for i, (st, mv) in enumerate(passes(ring_h[:, slot, w], ring_l[:, slot, w],
                                                            mid_h[:, mid, cols], mid_l[:, mid, cols])):
                            last = nc.tensor.matmul(pdn[:, n % BANKS, :], st, mv, start=j == 0 and i == 0,
                                                    stop=j == 1 and i == 2)
                            if n == 0 and j == 0 and i == 0:
                                last.then_inc(unit_used, 1)
                        if n == 15 and j == 0:
                            last.then_inc(unit_used, 1)
                    last.then_inc(down_done, 1)

            def column_sums(k, dst, c0, c1):
                pe.wait_ge(acc_done, adds_before(k + 1))
                parts = [acc]
                if ADDS[k] < KC - 1:
                    pe.wait_ge(sq_done, (k + 1) * KC)
                    parts.append(t_a)
                for j in range(c0, c1):
                    for part in parts:
                        last = nc.tensor.matmul(dst[:, j - c0:j - c0 + 1], part[:, j * P:(j + 1) * P],
                                                ones[:, 0:1], start=part is acc, stop=part is parts[-1])
                last.then_inc(colsum_done, 1)

            def spread(k, dst, c0, c1):
                pe.wait_ge(diag_done, k)
                for b in range((c1 - c0) * P // HALF):
                    cols = slice(c0 * P + b * HALF, c0 * P + (b + 1) * HALF)
                    last = nc.tensor.matmul(dst[:, b, :], ones[:], t_a[:, cols], start=True, stop=True)
                last.then_inc(bcast_done, 1)

            def first_two(norm, spread_k, u, q):
                project(u, u, q, in_pair(q), lambda k: pe.wait_ge(xs_ready, norm * KC + k + 1))
                column_sums(norm, pdn[:, 0, :], 0, KC)
                project(u + 1, u + 1, q + 1, in_pair(q + 1),
                        lambda k: spread(spread_k, pdn[:, 0:2, :], 0, KC) if k == 4 else None)

            def ffn(layer, norm, spread_k, last_banks):
                U, Q, N, A = FFN_U[layer], FFN_Q[layer], FFN_N[layer], FFN_A[layer]
                first_two(norm, spread_k, U, Q)
                project(U + 2, U + 2, Q + 2, in_pair(Q + 2))
                project(U + 3, U + 3, Q + 3, in_pair(Q + 3))
                with pe.Fori(0, (FG - 1) // 2) as i:
                    for odd in (1, 2):
                        g = i * 2 + odd
                        for j in range(4):
                            project(ffn_in_unit(layer, g) + j, U - 2 + 6 * odd + j, g * 4 + (Q + j),
                                    pin[:, 2 * (j % 2):2 * (j % 2) + 2, :])
                        down(ffn_down_unit(layer, g - 1), U + 2 + 6 * odd, i * 4 + (A + 2 * (odd - 1)),
                             i * 32 + (N + 16 * (odd - 1)), odd - 1)
                last = U + 3 * FC - 2
                last_banks(last, A + FC - 2, N + 16 * (FG - 1), FG - 1)

            pe.wait_ge(ones_set, 1)
            for n, (u, k) in enumerate(start_steps()):
                if k in (0, 4):
                    pe.wait_ge(start_ready, u + 1 + k // 2)
                if u == 0:
                    pe.wait_ge(xs_ready, k + 1)
                after_unit_0 = (u, k) == (1, KC - 2)
                project_chunk(u, in_pair(u), k, after_unit_0, in_done if k == KC - 1 else None)

            def start_norm(k):
                if k == 0:
                    column_sums(NORM_CONV, pdn[:, 0, :], 0, KC)
                if k == 4:
                    spread(1, pdn[:, 0:2, :], 0, KC)

            for g in range(CG):
                for j in range(6):
                    if g or j >= 2:
                        u, q = conv_in_unit(g) + j, 6 * g + j
                        project(u, u, q, in_pair(q), start_norm if q == 2 else None)
                if g:
                    down(conv_down_unit(g - 1), conv_down_unit(g - 1), CONV_A + 2 * (g - 1), 16 * (g - 1), g - 1)
            down(conv_down_unit(CG - 1), conv_down_unit(CG - 1), CONV_A + KC - 2, 16 * (CG - 1), CG - 1)

            ffn(0, NORM_FFN0, 2, lambda u, a, base, odd: down(u, u, a, base, odd))

            def feature_transform(g):
                pe.wait_ge(xs_ready, NORM_FOUR * KC + g + 1)
                for c in range(KC):
                    if g and c == 0:
                        pe.wait_ge(z_lo, g)
                    if g and c == 4:
                        pe.wait_ge(z_hi, g)
                    rows = slice(c * P, (c + 1) * P)
                    for i, (st, mv) in enumerate(passes(xs_h[:, g, rows], xs_l[:, g, rows],
                                                        feat_h[:], feat_l[:])):
                        last = nc.tensor.matmul(pin[:, c // 2, (c % 2) * 256:(c % 2 + 1) * 256], st, mv,
                                                start=i == 0, stop=i == 2)
                        if g == 0 and c == 0 and i == 0:
                            last.then_inc(unit_used, 1)
                    if c % 4 == 3:
                        last.then_inc(z_done, 1)

            def position_transform(g):
                if g >= 2:
                    pe.wait_ge(y_made, g - 1)
                for fold in range(2):
                    pe.wait_ge(fold_ready, 2 * g + fold + 1)
                    mid = 2 * (g % 2) + fold
                    for wave in range(2):
                        t = 2 * fold + wave
                        table = (FOUR_U + t) % RING
                        out = pdn[:, 2 * (g % 2) + wave, fold * 256:(fold + 1) * 256]
                        for c in range(4):
                            if t == 1 and c == 1:
                                for b in range(4):
                                    cos = slice(b * 256, b * 256 + P)
                                    for z in (mid_h[:, mid, cos], mid_l[:, mid, cos]):
                                        nc.tensor.matmul(out[:, 0:2], z, alt[:], start=False, stop=False)
                            st = slice(c * 256 + wave * P, c * 256 + (wave + 1) * P)
                            mv = slice(c * 256, (c + 1) * 256)
                            for i, (z, w) in enumerate(passes(mid_h[:, mid, st], mid_l[:, mid, st],
                                                              ring_h[:, table, mv], ring_l[:, table, mv])):
                                last = nc.tensor.matmul(out, z, w, start=c == 0 and i == 0,
                                                        stop=c == 3 and i == 2)
                        if g == KC - 1 and t < 3:
                            last.then_inc(unit_used, 1)
                last.then_inc(y_done, 1)

            pe.wait_ge(feat_ready, 1)
            pe.wait_ge(alt_ready, 1)
            feature_transform(0)
            column_sums(NORM_FOUR, pdn[:, 0, :], 0, KC)
            pe.wait_ge(unit_ready, FOUR_U + 4 - BY_START)
            for g in range(KC):
                if g < KC - 1:
                    feature_transform(g + 1)
                position_transform(g)
            for m in range(KC):
                u = FOUR_U + 4 + m
                project(u, u, FOUR_Q + m, in_pair(FOUR_Q + m),
                        (lambda k: pe.wait_ge(y_ready, k + 1)) if m == 0 else None,
                        y_spent if m == KC - 1 else None)

            def last_banks(u, a, base, odd):
                down(u, u, a, base, odd, range(0, 12), True)
                column_sums(NORM_FINAL, pin[:, 0, :], 0, 4)
                down(u, u, a, base, odd, range(12, 14), True)
                spread(4, pin[:, 1:2, :], 0, 4)
                down(u, u, a, base, odd, range(14, 16), True)
                column_sums(NORM_FINAL + 1, pin[:, 2, :], 4, 8)
                spread(5, pin[:, 3:4, :], 4, 8)

            ffn(1, NORM_FFN1, 3, last_banks)


def dft_tables():
    import numpy as np

    s = np.arange(S // 2)[:, None]
    j = np.arange(S // 4)[None, :]
    even = 2 * np.pi * ((s * 2 * j) % S) / S
    odd = 2 * np.pi * ((s * (2 * j + 1)) % S) / S
    waves = [np.cos(even), np.sin(even), np.cos(odd), np.sin(odd)]
    waves[1][:, 0] = 0.0
    seq = np.stack([w.reshape(4, P, S // 4).transpose(1, 0, 2).reshape(P, D) for w in waves]) * S ** -0.5
    d = np.arange(P)
    turn = 2 * np.pi * ((d[:, None] * d[None, :]) % P) / P
    feat = np.concatenate([np.cos(turn), np.sin(turn)], axis=1) * P ** -0.5
    cst = np.zeros((P, P + 2))
    cst[:, 0:P] = np.eye(P)
    cst[:, P] = (1.0 - 2.0 * (d % 2)) * S ** -0.5
    return [a.astype(np.float32) for a in (seq.reshape(4 * P, D), feat, cst)]


def kernel(x, conv_w_in, conv_k, conv_w_out, fourier_w_out, mix_norm_g, ffn_norm_g, ffn_w_gate, ffn_w_up,
           ffn_w_down, final_norm_g):
    import numpy as np
    import concourse.bacc as bacc
    from concourse.bass_utils import run_bass_kernel_spmd

    def column_units(w):
        w = np.asarray(w)
        n = w.shape[-1] // P
        w = w.reshape(-1, KC, P, n, P).transpose(0, 3, 2, 1, 4)
        return np.ascontiguousarray(w.reshape(-1, D))

    gains = [mix_norm_g[0], ffn_norm_g[0], mix_norm_g[1], ffn_norm_g[1], final_norm_g]
    gains = np.stack([np.asarray(g) for g in gains]).reshape(5, KC, P).transpose(2, 0, 1)
    taps = np.asarray(conv_k)[0].reshape(3, KC, P).transpose(2, 0, 1)
    seq, feat, cst = dft_tables()
    arrays = {
        "xT": np.ascontiguousarray(np.asarray(x)[0].T),
        "w_in": column_units(conv_w_in),
        "w_conv": np.ascontiguousarray(np.asarray(conv_w_out)[0]),
        "w_four": column_units(fourier_w_out),
        "w_gate": column_units(ffn_w_gate),
        "w_up": column_units(ffn_w_up),
        "w_down": np.ascontiguousarray(np.asarray(ffn_w_down).reshape(2 * FF, D)),
        "gains": np.ascontiguousarray(gains),
        "taps": np.ascontiguousarray(taps),
        "seq": seq,
        "feat": feat,
        "cst": cst,
    }
    nc = bacc.Bacc("TRN2", target_bir_lowering=False, num_devices=1)
    args = [nc.dram_tensor(name + "_dram", a.shape, mybir.dt.float32, kind="ExternalInput").ap()
            for name, a in arrays.items()]
    out = nc.dram_tensor("out_dram", (D, S), mybir.dt.float32, kind="ExternalOutput").ap()
    build(nc, *args, out)
    result = run_bass_kernel_spmd(nc, [{name + "_dram": a for name, a in arrays.items()}], core_ids=[0])
    return np.ascontiguousarray(result.results[0]["out_dram"].T).reshape(1, S, D)
```

```python
import concourse.bass as bass
from concourse import mybir
from contextlib import ExitStack

P = 128
D = 1024
S = 1024
KC = D // P
HALF = 512
FF = 2816
FC = FF // P
FG = FC // 2
CG = KC // 2
RMS_EPS = 1e-5
RAW = 3
RING = 6
ACTS = 4
E = P // 2
PAIRS = KC // 2
Q = S // 4
EDGE_COLS = 72
BANKS = 4
BY_START = 2
FINAL_HALVES = ((0, 4), (4, 8))
FINAL_DVE = 6
STORE_ORDER = ((0, 1, 2, 3, 4, 6, 7, 5), (0, 1, 6, 2, 3, 7, 4, 5))
UNITS_IN_PAIR = 12

CONV_U = 0
FFN_U = [CONV_U + 4 * KC, 0]
FOUR_U = FFN_U[0] + 3 * FC
FFN_U[1] = FOUR_U + 4 + KC
CONV_Q = 0
FFN_Q = [CONV_Q + 3 * KC, CONV_Q + 3 * KC + 2 * FC + KC]
FOUR_Q = FFN_Q[0] + 2 * FC
CONV_N = 0
FFN_N = [16 * CG, 16 * (CG + FG)]
CONV_A = 0
FFN_A = [KC, KC + FC]
NORM_CONV, NORM_FFN0, NORM_FOUR, NORM_FFN1, NORM_FINAL = range(5)
ADDS = [KC - 1, KC - 1, KC - 2, KC - 1] + [KC - 2] * 2


def half_cols(h):
    return slice(FINAL_HALVES[h][0] * P, FINAL_HALVES[h][1] * P)


def adds_before(norm):
    return sum(ADDS[:norm])


def conv_in_unit(g):
    return CONV_U + (0 if g == 0 else 8 * g - 2)


def conv_down_unit(g):
    return CONV_U + (8 * g + 12 if g < CG - 1 else 4 * KC - 2)


def ffn_in_unit(layer, g):
    return g * 6 + (FFN_U[layer] - 2)


def ffn_down_unit(layer, g):
    return g * 6 + (FFN_U[layer] + 8)


def start_steps():
    steps = [(0, 0)]
    for k in range(1, KC):
        steps += [(0, k), (1, k - 1)]
    return steps + [(1, KC - 1)]


def build(nc, xT, w_in, w_conv, w_four, w_gate, w_up, w_down, gains_d, taps_d, seq_d, feat_d, cst_d, outT):
    F32 = mybir.dt.float32
    F32R = mybir.dt.float32r
    ALU = mybir.AluOpType
    ACT = mybir.ActivationFunctionType

    ctx = ExitStack()
    with ctx:
        def sb(name, shape, dt=F32):
            return ctx.enter_context(nc.sbuf_tensor(name, shape, dt))

        def sem(name):
            return ctx.enter_context(nc.semaphore(name))

        res = sb("res", [P, KC, S])
        xs_h = sb("xs_h", [P, KC, S], F32R)
        xs_l = sb("xs_l", [P, KC, S], F32R)
        mid_h = sb("mid_h", [P, ACTS, S], F32R)
        mid_l = sb("mid_l", [P, ACTS, S], F32R)
        edge_h = sb("edge_h", [P, P], F32R)
        edge_l = sb("edge_l", [P, P], F32R)
        raw = sb("raw", [P, RAW, D])
        ring_h = sb("ring_h", [P, RING, D], F32R)
        ring_l = sb("ring_l", [P, RING, D], F32R)
        t_a = sb("t_a", [P, S])
        t_b = sb("t_b", [P, S])
        padded = sb("padded", [P, S + 2])
        acc = padded[:, 1:S + 1]
        wide = sb("wide", [P, S + 2])
        rb = wide[:, 0:S]
        gains = sb("gains", [P, 5, KC])
        taps = sb("taps", [P, 3, KC])
        cst = sb("cst", [P, P + 4])
        ident = cst[:, 0:P]
        ones = sb("ones", [P, P])
        feat = sb("feat", [P, 5 * E], F32R)
        alt = sb("alt", [P, 2], F32R)
        stat = sb("stat", [P, KC])
        root = sb("root", [P, KC])
        step = sb("step", [P, KC])
        rcol = sb("rcol", [P, KC])

        pin = ctx.enter_context(nc.psum_tensor("pin", [P, 4, HALF], F32))
        pdn = ctx.enter_context(nc.psum_tensor("pdn", [P, BANKS, HALF], F32))

        def in_pair(q):
            return pdn[:, 2:4, :] if q == 2 else pin[:, 2 * (q % 2):2 * (q % 2) + 2, :]

        def final_sums(h):
            return pin[:, 2 * h, 0:KC]

        def final_spread_bank(h):
            return pin[:, 2 * h + 1, :]

        def feature_banks(g):
            return pdn if g == 1 else pin

        def computed(banks, first, end):
            return banks[:].rearrange("p b (c n) -> p (b c) n", c=2)[:, first:end, :].rearrange(
                "p c (w n) -> p c w n", w=2)[:, :, :, 0:E]

        def of_group(t, g):
            return t[:].rearrange("p (c w g e) -> p c w g e", w=2, g=2, e=E)[:, :, :, g % 2, :]

        raw_landed = [sem(f"raw_landed{i}") for i in range(RAW)]
        start_landed = [sem(f"start_landed{i}") for i in range(BY_START)]
        start_high = sem("start_high")
        start_ready = sem("start_ready")
        unit_high = sem("unit_high")
        unit_ready = sem("unit_ready")
        unit_used = sem("unit_used")
        x_landed = [sem(f"x_landed{i}") for i in range(KC)]
        x_first = sem("x_first")
        x_first_high = sem("x_first_high")
        x_first_ready = sem("x_first_ready")
        gains_landed = sem("gains_landed")
        small_landed = sem("small_landed")
        feat_landed = sem("feat_landed")
        feat_high = sem("feat_high")
        feat_ready = sem("feat_ready")
        feat_pad = sem("feat_pad")
        ones_set = sem("ones_set")
        alt_ready = sem("alt_ready")
        edges_set = sem("edges_set")
        xs_high = sem("xs_high")
        xs_ready = sem("xs_ready")
        sq_done = sem("sq_done")
        acc_done = sem("acc_done")
        colsum_done = sem("colsum_done")
        stat_done = sem("stat_done")
        root_done = sem("root_done")
        newton = sem("newton")
        rcol_ready = sem("rcol_ready")
        diag_done = sem("diag_done")
        bcast_done = sem("bcast_done")
        rb_ready = sem("rb_ready")
        in_done = sem("in_done")
        in_free = sem("in_free")
        gate2 = sem("gate2")
        tap_mid = sem("tap_mid")
        tap_left = sem("tap_left")
        tap_right = sem("tap_right")
        silu_done = sem("silu_done")
        mid_made = sem("mid_made")
        mid_high = sem("mid_high")
        mid_ready = sem("mid_ready")
        down_done = sem("down_done")
        down_added = sem("down_added")
        z_done = sem("z_done")
        z_lo = sem("z_lo")
        z_hi = sem("z_hi")
        plus_made = sem("plus_made")
        minus_made = sem("minus_made")
        plus_high = sem("plus_high")
        minus_high = sem("minus_high")
        fold_ready = sem("fold_ready")
        edge_zero = sem("edge_zero")
        edge_ready = sem("edge_ready")
        edge_done = sem("edge_done")
        edge_taken = sem("edge_taken")
        edge_made = sem("edge_made")
        edge_high = sem("edge_high")
        edge_low = sem("edge_low")
        edges_landed = sem("edges_landed")
        last_edge_landed = sem("last_edge_landed")
        y_last = sem("y_last")
        y_done = sem("y_done")
        y_cos = sem("y_cos")
        y_made = sem("y_made")
        y_high = sem("y_high")
        y_ready = sem("y_ready")
        y_spent = sem("y_spent")
        gained = sem("gained")
        scaled = [sem("scaled_dve"), sem("scaled_pool")]
        stored = sem("stored")

        block = ctx.enter_context(nc.Block())

        @block.sync
        def _(sp):
            def load_unit(u, slot_of, src):
                if isinstance(u, int) and u - RAW < BY_START:
                    if u >= RAW:
                        sp.wait_ge(start_ready, 2 + u - RAW + 1)
                else:
                    sp.wait_ge(unit_ready, u - (RAW - 1 + BY_START))
                sp.dma_start(raw[:, slot_of % RAW, :], src).then_inc(raw_landed[slot_of % RAW], 16)

            def col_rows(w, f):
                return w[bass.ds(f * P, P), :]

            def conv_in(g):
                u = conv_in_unit(g)
                for j in range(2):
                    for part in (1, 2, 0):
                        load_unit(u, u, col_rows(w_in, part * KC + 2 * g + j))
                        u += 1

            def conv_down(g):
                for j in range(2):
                    u = conv_down_unit(g) + j
                    load_unit(u, u, col_rows(w_conv, 2 * g + j))

            def ffn_in(layer, g, u, slot):
                for j in range(2):
                    for w in (w_gate, w_up):
                        load_unit(u, slot, col_rows(w, g * 2 + (layer * FC + j)))
                        u, slot = u + 1, slot + 1

            def ffn_down(layer, g, u, slot):
                for j in range(2):
                    load_unit(u + j, slot + j, col_rows(w_down, g * 2 + (layer * FC + j)))

            def ffn(layer):
                ffn_in(layer, 0, FFN_U[layer], FFN_U[layer])
                with sp.Fori(0, (FG - 1) // 2) as i:
                    for odd in (1, 2):
                        g = i * 2 + odd
                        ffn_in(layer, g, ffn_in_unit(layer, g), FFN_U[layer] - 2 + 6 * odd)
                        ffn_down(layer, g - 1, ffn_down_unit(layer, g - 1), FFN_U[layer] + 2 + 6 * odd)
                last = FFN_U[layer] + 3 * FC - 2
                ffn_down(layer, FG - 1, last, last)

            def load_x(first, end):
                for m in range(first, end):
                    sp.dma_start(res[:, m, :], xT[m * P:(m + 1) * P, :]).then_inc(x_landed[m], 16)

            def load_x_first(half, landed):
                cols = slice(half * HALF, (half + 1) * HALF)
                sp.dma_start(res[:, 0, cols], xT[0:P, cols]).then_inc(landed, 16)

            def load_start(u, half):
                cols = slice(half * D // 2, (half + 1) * D // 2)
                landed = raw_landed[u] if half else start_landed[u]
                sp.dma_start(raw[:, u, cols], col_rows(w_in, (u + 1) * KC)[:, cols]).then_inc(landed, 16)

            load_x_first(0, x_first)
            load_start(0, 0)
            load_x_first(1, x_landed[0])
            load_start(1, 0)
            load_x(1, 3)
            load_start(0, 1)
            load_start(1, 1)
            load_x(3, KC)
            for g in range(CG):
                if g == 0:
                    rest = [(0, 0), (1, 1), (1, 2), (1, 0)]
                    for n, (j, part) in enumerate(rest):
                        load_unit(BY_START + n, BY_START + n, col_rows(w_in, part * KC + j))
                else:
                    conv_in(g)
                    conv_down(g - 1)
            conv_down(CG - 1)
            ffn(0)
            for t in range(4):
                load_unit(FOUR_U + t, FOUR_U + t, seq_d[t * P:(t + 1) * P, :])
            for m in range(KC):
                load_unit(FOUR_U + 4 + m, FOUR_U + 4 + m, col_rows(w_four, m))
            ffn(1)
            for h, order in enumerate(STORE_ORDER):
                for m in order:
                    if m < FINAL_DVE:
                        sp.wait_ge(scaled[0], h * FINAL_DVE + m + 1)
                    else:
                        sp.wait_ge(scaled[1], h * (KC - FINAL_DVE) + m - FINAL_DVE + 1)
                    sp.dma_start(outT[m * P:(m + 1) * P, half_cols(h)], res[:, m, half_cols(h)]).then_inc(stored, 16)
            sp.wait_ge(stored, 16 * 2 * KC)

        @block.gpsimd
        def _(pool):
            def split_unit(u, slot_of, landed, low=True):
                pool.wait_ge(raw_landed[slot_of % RAW], landed * 16)
                if not isinstance(u, int) or u >= RING:
                    pool.wait_ge(unit_used, u - (RING - 1))
                src = raw[:, slot_of % RAW, :]
                high = ring_h[:, slot_of % RING, :]
                blocks = [ap.rearrange("p (c n) -> p c n", n=P) for ap in (high, src)]
                one = ones[:].rearrange("p (c n) -> p c n", c=1).to_broadcast([P, KC, P])
                nc.gpsimd.tensor_tensor(blocks[0], blocks[1], one, ALU.mult).then_inc(unit_high, 1)
                if not low:
                    return
                pool.wait_ge(unit_high, u + (1 - BY_START))
                nc.gpsimd.tensor_tensor(ring_l[:, slot_of % RING, :], src, high.bitcast(F32),
                                        ALU.subtract).then_inc(unit_ready, 1)

            def split_units(first, end):
                for u in range(first, end):
                    split_unit(u, u, u // RAW + 1)

            def add_square(norm, m):
                pool.wait_ge(sq_done, norm * KC + m + 1)
                if m >= 2:
                    pool.wait_ge(acc_done, adds_before(norm) + m - 1)
                sq = t_a if m % 2 else t_b
                nc.gpsimd.tensor_tensor(acc, acc, sq[:], ALU.add).then_inc(acc_done, 1)

            def ffn(layer):
                first = FFN_U[layer] + 4
                with pool.Fori(0, (FG - 1) // 2) as i:
                    for j in range(UNITS_IN_PAIR):
                        u = first + j
                        split_unit(i * UNITS_IN_PAIR + u, u, i * (UNITS_IN_PAIR // RAW) + (u // RAW + 1))
                split_units(FFN_U[layer] + 3 * FC - 2, FFN_U[layer] + 3 * FC)

            nc.gpsimd.memset(ones[:], 1.0).then_inc(ones_set, 1)
            nc.gpsimd.memset(padded[:, 0:1], 0.0).then_inc(edges_set, 1)
            nc.gpsimd.memset(feat[:, 4 * E:5 * E].bitcast(F32), 0.0).then_inc(feat_pad, 1)
            nc.gpsimd.memset(edge_h[:, E:P].bitcast(F32), 0.0).then_inc(edge_zero, 1)
            nc.gpsimd.memset(edge_l[:, E:P].bitcast(F32), 0.0).then_inc(edge_zero, 1)
            nc.gpsimd.memset(padded[:, S + 1:S + 2], 0.0).then_inc(edges_set, 1)
            pool.wait_ge(ones_set, 1)
            for m in range(1, KC):
                add_square(NORM_CONV, m)
                if m == 6:
                    split_unit(BY_START, BY_START, 1, low=False)
            pool.wait_ge(feat_landed, 16)
            table = feat[:, 0:4 * E].rearrange("p (w i e) -> p w i e", w=2, i=2)
            waves = rb[:, 0:P].rearrange("p (w e) -> p w e", w=2)
            nc.gpsimd.tensor_copy(table[:, :, 0, :], waves).then_inc(feat_high, 1)
            pool.wait_ge(feat_high, 1)
            nc.gpsimd.tensor_tensor(table[:, :, 1, :], waves, table[:, :, 0, :].bitcast(F32),
                                    ALU.subtract).then_inc(feat_ready, 1)
            pool.wait_ge(unit_ready, 1)
            split_units(BY_START + 1, FFN_U[0] + 4)
            for m in range(1, KC):
                add_square(NORM_FFN0, m)
            ffn(0)
            split_units(FOUR_U, FOUR_U + 4)
            for m in range(1, KC - 1):
                add_square(NORM_FOUR, m)
            split_units(FOUR_U + 4, FOUR_U + 6)
            for k in range(KC - 2):
                pool.wait_ge(y_high, k + 1)
                y = wide[:, S:0:-1] if k % 2 else rb
                nc.gpsimd.tensor_tensor(xs_l[:, k, :], y, xs_h[:, k, :].bitcast(F32),
                                        ALU.subtract).then_inc(y_ready, 1)
            split_units(FOUR_U + 6, FOUR_U + 10)
            for m in range(KC):
                if m:
                    add_square(NORM_FFN1, m)
                if m < 6:
                    split_units(FOUR_U + 10 + m, FOUR_U + 11 + m)
            ffn(1)
            for h in range(2):
                cols = half_cols(h)
                for m in range(1, KC - 1):
                    pool.wait_ge(sq_done, (NORM_FINAL + h) * KC + m + 1)
                    if m >= 2:
                        pool.wait_ge(acc_done, adds_before(NORM_FINAL + h) + m - 1)
                    sq = t_a if m % 2 else t_b
                    nc.gpsimd.tensor_tensor(acc[:, cols], acc[:, cols], sq[:, cols],
                                            ALU.add).then_inc(acc_done, 1)
            for h in range(2):
                cols = half_cols(h)
                pool.wait_ge(rb_ready, 4 + h)
                for m in range(FINAL_DVE, KC):
                    pool.wait_ge(gained, (KC - FINAL_DVE) * h + m - FINAL_DVE + 1)
                    nc.gpsimd.tensor_tensor(res[:, m, cols], res[:, m, cols], rb[:, cols],
                                            ALU.mult).then_inc(scaled[1], 1)

        @block.scalar
        def _(act):
            def norm_high(norm, m, cols=slice(0, S), done=xs_high):
                nc.scalar.activation(xs_h[:, m, cols], res[:, m, cols], ACT.Copy,
                                     scale=gains[:, norm, m:m + 1]).then_inc(done, 1)

            def norm_square(norm, m):
                if m >= 3:
                    act.wait_ge(acc_done, adds_before(norm) + m - 2)
                sq = acc if m == 0 else t_a[:] if m % 2 else t_b[:]
                nc.scalar.activation(sq, res[:, m, :], ACT.Square).then_inc(sq_done, 1)

            def norm_feed(norm, wait_chunk):
                nc.scalar.preload_act_table(ACT.Sqrt)
                for m in range(KC):
                    wait_chunk(m)
                    norm_square(norm, m)
                    norm_high(norm, m)

            def norm_root(k, c0, c1):
                act.wait_ge(stat_done, k + 1)
                nc.scalar.activation(root[:, c0:c1], stat[:, c0:c1], ACT.Sqrt).then_inc(root_done, 1)

            def norm_spread(k, c0, c1):
                act.wait_ge(bcast_done, k)
                n = (c1 - c0) // HALF
                nc.scalar.activation(rb[:, c0:c1], pdn[:, 0:n, :], ACT.Copy).then_inc(rb_ready, 1)

            def mid_round(a, slot):
                act.wait_ge(mid_made, a + 1)
                nc.scalar.activation(mid_h[:, slot, :], t_b[:], ACT.Copy).then_inc(mid_high, 1)

            def conv_chunk(f):
                act.wait_ge(in_free, 3 * f + 2)
                nc.scalar.activation(t_a[:], acc, ACT.Copy, scale=taps[:, 1, f:f + 1]).then_inc(tap_mid, 1)
                mid_round(f, f % ACTS)

            def ffn_group(layer, g, odd):
                for j in range(2):
                    act.wait_ge(in_free, g * 4 + (FFN_Q[layer] + 2 * j + 1))
                    nc.scalar.activation(t_a[:], t_a[:], ACT.Silu).then_inc(silu_done, 1)
                    mid_round(g * 2 + (FFN_A[layer] + j), 2 * (odd % 2) + j)

            def ffn(layer):
                ffn_group(layer, 0, 0)
                with act.Fori(0, (FG - 1) // 2) as i:
                    for odd in (1, 2):
                        ffn_group(layer, i * 2 + odd, odd)

            def last_down(base, norm):
                def wait_chunk(m):
                    act.wait_ge(down_added, base + 2 * m + 2)
                norm_feed(norm, wait_chunk)

            nc.scalar.preload_act_table(ACT.Sqrt)
            act.dma_start(gains[:], gains_d).then_inc(gains_landed, 16)
            act.dma_start(taps[:], taps_d).then_inc(small_landed, 16)
            act.dma_start(cst[:], cst_d).then_inc(small_landed, 16)
            act.dma_start(rb[:, 0:P], feat_d).then_inc(feat_landed, 16)
            act.wait_ge(gains_landed, 16)

            def start_unit_high(u, half):
                act.wait_ge(raw_landed[u] if half else start_landed[u], 16)
                cols = slice(half * D // 2, (half + 1) * D // 2)
                nc.scalar.activation(ring_h[:, u, cols], raw[:, u, cols], ACT.Copy).then_inc(start_high, 1)

            act.wait_ge(x_first, 16)
            norm_high(NORM_CONV, 0, slice(0, HALF), x_first_high)
            start_unit_high(0, 0)
            act.wait_ge(x_landed[0], 16)
            norm_high(NORM_CONV, 0, slice(HALF, S))
            start_unit_high(1, 0)
            norm_square(NORM_CONV, 0)
            for m in range(1, KC):
                act.wait_ge(x_landed[m], 16)
                norm_high(NORM_CONV, m)
                if m == 2:
                    for u in range(BY_START):
                        start_unit_high(u, 1)
                norm_square(NORM_CONV, m)
            act.wait_ge(small_landed, 16 * 2)
            nc.scalar.activation(alt[:], cst[:, P:P + 2], ACT.Copy).then_inc(alt_ready, 1)
            norm_root(NORM_CONV, 0, KC)
            act.wait_ge(feat_ready, 1)
            norm_spread(NORM_CONV + 1, 0, S)
            for f in range(KC):
                conv_chunk(f)
            act.wait_ge(mid_ready, CONV_A + KC)
            last_down(CONV_N + 16 * (CG - 1), NORM_FFN0)
            norm_root(NORM_FFN0, 0, KC)
            norm_spread(NORM_FFN0 + 1, 0, S)
            ffn(0)
            act.wait_ge(mid_ready, FFN_A[0] + FC)
            last_down(FFN_N[0] + 16 * (FG - 1), NORM_FOUR)
            norm_root(NORM_FOUR, 0, KC)
            act.wait_ge(rcol_ready, NORM_FOUR + 1)

            def cosine_sums(dst, bank):
                nc.scalar.activation(dst.rearrange("p (j e) -> p j e", e=2),
                                     bank.rearrange("p (e j) -> p j e", e=2), ACT.Copy)

            def evacuate(g):
                act.wait_ge(z_done, 2 * g + 1)
                if g % 2 == 0 and g:
                    act.wait_ge(fold_ready, g)
                for c in range(4):
                    last = nc.scalar.activation(of_group(t_a, g)[:, c], computed(feature_banks(g), c, c + 1)[:, 0],
                                                ACT.Copy, scale=rcol[:, c:c + 1])
                last.then_inc(z_lo, 1)

            def fold_high(p):
                act.wait_ge(plus_made, p + 1)
                nc.scalar.activation(mid_h[:, 2 * (p % 2), :], acc, ACT.Copy).then_inc(plus_high, 1)
                act.wait_ge(minus_made, p + 1)
                nc.scalar.activation(mid_h[:, 2 * (p % 2) + 1, :], t_a[:], ACT.Copy).then_inc(minus_high, 1)

            def y_cosines(p):
                act.wait_ge(y_done, p + 1)
                if p:
                    act.wait_ge(y_ready, 2 * p)
                bank = 2 * (p % 2)
                cosine_sums(rb[:, 0:HALF], pdn[:, bank, :])
                nc.scalar.activation(wide[:, S:S + 1], pdn[:, bank, 0:1], ACT.Copy).then_inc(y_cos, 1)

            def y_highs(p):
                act.wait_ge(y_made, p + 1)
                nc.scalar.activation(xs_h[:, 2 * p, :], rb, ACT.Copy).then_inc(y_high, 1)
                nc.scalar.activation(xs_h[:, 2 * p + 1, :], wide[:, S:0:-1], ACT.Copy).then_inc(y_high, 1)

            evacuate(0)
            for p in range(PAIRS):
                evacuate(2 * p + 1)
                fold_high(p)
                if p:
                    y_cosines(p - 1)
                if p < PAIRS - 1:
                    evacuate(2 * p + 2)
                if p:
                    y_highs(p - 1)
            act.wait_ge(edge_done, 1)
            cosine_sums(t_b[0:KC, 0:HALF], pin[0:KC, 0, :])
            nc.scalar.activation(t_b[0:KC, S // 2:S // 2 + 1], pin[0:KC, 1, 0:1], ACT.Copy).then_inc(edge_taken, 1)
            act.wait_ge(edge_made, 1)
            nc.scalar.activation(mid_h[0:KC, 0, :], t_b[0:KC, :], ACT.Copy).then_inc(edge_high, 1)
            act.wait_ge(edge_low, 1)

            def place_edges(first, end, landed):
                for src, dst in ((mid_h, xs_h), (mid_l, xs_l)):
                    for odd in range(2):
                        rows = src[PAIRS * odd + first:PAIRS * odd + end, 0, :]
                        act.dma_start(dst[E * odd:E * odd + 1, 2 * first + 1:2 * end:2, :].bitcast(F32),
                                      rows.bitcast(F32)).then_inc(landed, 16)

            act.wait_ge(y_ready, KC - 2)
            place_edges(0, PAIRS - 1, edges_landed)
            y_cosines(PAIRS - 1)
            y_highs(PAIRS - 1)
            act.wait_ge(y_last, 2)
            place_edges(PAIRS - 1, PAIRS, last_edge_landed)

            for m in range(KC):
                act.wait_ge(in_free, FOUR_Q + m + 1)
                norm_square(NORM_FFN1, m)
                if m == KC - 2:
                    for k in range(KC - 1):
                        act.wait_ge(y_spent, k + 1)
                        norm_high(NORM_FFN1, k)
            act.wait_ge(in_done, FOUR_Q + KC)
            norm_high(NORM_FFN1, KC - 1)
            norm_root(NORM_FFN1, 0, KC)
            norm_spread(NORM_FFN1, 0, S)
            ffn(1)
            def final_squares(h, first, end):
                cols = half_cols(h)
                for m in range(first, end):
                    act.wait_ge(down_added, FFN_N[1] + 16 * (FG - 1) + KC * h + m + 1)
                    if m >= 3:
                        act.wait_ge(acc_done, adds_before(NORM_FINAL + h) + m - 2)
                    sq = acc if m == 0 else t_a if m % 2 else t_b
                    nc.scalar.activation(sq[:, cols], res[:, m, cols], ACT.Square).then_inc(sq_done, 1)

            def final_spread(h):
                act.wait_ge(bcast_done, NORM_FINAL + h)
                nc.scalar.activation(rb[:, half_cols(h)], final_spread_bank(h), ACT.Copy).then_inc(rb_ready, 1)

            act.wait_ge(mid_ready, FFN_A[1] + FC)
            nc.scalar.preload_act_table(ACT.Sqrt)
            final_squares(0, 0, KC)
            final_squares(1, 0, 4)
            norm_root(NORM_FINAL, *FINAL_HALVES[0])
            final_squares(1, 4, 6)
            final_spread(0)
            final_squares(1, 6, KC)
            norm_root(NORM_FINAL + 1, *FINAL_HALVES[1])
            final_spread(1)

        @block.vector
        def _(dve):
            def norm_low(norm, m, cols=slice(0, S), done=xs_ready):
                if done is xs_ready:
                    dve.wait_ge(xs_high, norm * KC + m + 1)
                nc.vector.scalar_tensor_tensor(xs_l[:, m, cols], res[:, m, cols], gains[:, norm, m:m + 1],
                                               xs_h[:, m, cols].bitcast(F32), ALU.mult,
                                               ALU.subtract).then_inc(done, 1)

            def norm_column(k, colsum, c0, c1):
                dve.wait_ge(colsum_done, k + 1)
                nc.vector.tensor_scalar(stat[:, c0:c1], colsum, 1.0 / D, RMS_EPS, ALU.mult,
                                        ALU.add).then_inc(stat_done, 1)
                dve.wait_ge(root_done, k + 1)
                nc.vector.reciprocal(rcol[:, c0:c1], root[:, c0:c1]).then_inc(newton, 1)
                dve.wait_ge(newton, 4 * k + 1)
                nc.vector.tensor_tensor(step[:, c0:c1], rcol[:, c0:c1], rcol[:, c0:c1], ALU.mult).then_inc(newton, 1)
                dve.wait_ge(newton, 4 * k + 2)
                nc.vector.tensor_tensor(step[:, c0:c1], step[:, c0:c1], stat[:, c0:c1], ALU.mult).then_inc(newton, 1)
                dve.wait_ge(newton, 4 * k + 3)
                nc.vector.tensor_scalar(step[:, c0:c1], step[:, c0:c1], -0.5, 1.5, ALU.mult, ALU.add).then_inc(newton, 1)
                dve.wait_ge(newton, 4 * k + 4)
                nc.vector.tensor_tensor(rcol[:, c0:c1], rcol[:, c0:c1], step[:, c0:c1], ALU.mult).then_inc(rcol_ready, 1)
                dve.wait_ge(rcol_ready, k + 1)

            def norm_diag(c0, c1):
                n = c1 - c0
                nc.vector.tensor_tensor(
                    t_a[:, c0 * P:c1 * P].rearrange("p (j n) -> p j n", n=P),
                    ident.rearrange("p (j n) -> p j n", j=1).to_broadcast([P, n, P]),
                    rcol[:, c0:c1].rearrange("p (j n) -> p j n", n=1).to_broadcast([P, n, P]),
                    ALU.mult).then_inc(diag_done, 1)

            def scale_out(q, pair, dst):
                dve.wait_ge(in_done, q + 1)
                nc.vector.tensor_tensor(dst, pair.rearrange("p b n -> p (b n)"), rb,
                                        ALU.mult).then_inc(in_free, 1)
                dve.wait_ge(in_free, q + 1)

            def mid_low(a, slot):
                dve.wait_ge(mid_high, a + 1)
                nc.vector.tensor_tensor(mid_l[:, slot, :], t_b[:], mid_h[:, slot, :].bitcast(F32),
                                        ALU.subtract).then_inc(mid_ready, 1)

            def down_add(n, m, h, bank):
                dve.wait_ge(down_done, n + 1)
                cols = slice(h * HALF, (h + 1) * HALF)
                nc.vector.tensor_tensor(res[:, m, cols], pdn[:, bank, :], res[:, m, cols],
                                        ALU.add).then_inc(down_added, 1)

            def down_adds(base, first, end):
                for n in range(first, end):
                    down_add(base + n, n // 2, n % 2, n % BANKS)

            def last_down(base, norm):
                for m in range(KC):
                    down_adds(base, 2 * m, 2 * m + 2)
                    if m:
                        norm_low(norm, m - 1)
                norm_low(norm, KC - 1)

            def conv_chunk(f, tail):
                q = 3 * f
                scale_out(q, in_pair(q), t_a[:])
                nc.vector.tensor_tensor(t_a[:], t_a[:], rb, ALU.mult).then_inc(gate2, 1)
                dve.wait_ge(gate2, f + 1)
                dve.wait_ge(in_done, q + 2)
                nc.vector.tensor_tensor(acc, in_pair(q + 1).rearrange("p b n -> p (b n)"),
                                        t_a[:], ALU.mult).then_inc(in_free, 1)
                dve.wait_ge(in_free, q + 2)
                dve.wait_ge(tap_mid, f + 1)
                nc.vector.scalar_tensor_tensor(t_a[:], padded[:, 0:S], taps[:, 0, f:f + 1], t_a[:],
                                               ALU.mult, ALU.add).then_inc(tap_left, 1)
                dve.wait_ge(tap_left, f + 1)
                nc.vector.scalar_tensor_tensor(t_a[:], padded[:, 2:S + 2], taps[:, 2, f:f + 1], t_a[:],
                                               ALU.mult, ALU.add).then_inc(tap_right, 1)
                dve.wait_ge(tap_right, f + 1)
                scale_out(q + 2, in_pair(q + 2), t_b[:])
                nc.vector.tensor_tensor(t_b[:], t_b[:], t_a[:], ALU.mult).then_inc(mid_made, 1)
                tail()
                mid_low(f, f % ACTS)

            def ffn_group(layer, g, odd, down_base):
                for j in range(2):
                    q = g * 4 + (FFN_Q[layer] + 2 * j)
                    a = g * 2 + (FFN_A[layer] + j)
                    scale_out(q, pin[:, 0:2, :], t_a[:])
                    scale_out(q + 1, pin[:, 2:4, :], t_b[:])
                    dve.wait_ge(silu_done, a - (KC - 1))
                    nc.vector.tensor_tensor(t_b[:], t_b[:], t_a[:], ALU.mult).then_inc(mid_made, 1)
                    if j and down_base is not None:
                        down_adds(down_base, 0, 2)
                    mid_low(a, 2 * (odd % 2) + j)
                if down_base is not None:
                    down_adds(down_base, 2, 16)

            def ffn(layer):
                ffn_group(layer, 0, 0, None)
                with dve.Fori(0, (FG - 1) // 2) as i:
                    for odd in (1, 2):
                        g = i * 2 + odd
                        ffn_group(layer, g, odd, i * 32 + (FFN_N[layer] + 16 * (odd - 1)))

            dve.wait_ge(gains_landed, 16)
            dve.wait_ge(edges_set, 2)
            def start_unit_low(u, n, half):
                dve.wait_ge(start_high, n)
                cols = slice(half * D // 2, (half + 1) * D // 2)
                nc.vector.tensor_tensor(ring_l[:, u, cols], raw[:, u, cols], ring_h[:, u, cols].bitcast(F32),
                                        ALU.subtract).then_inc(start_ready, 1)

            dve.wait_ge(x_first_high, 1)
            norm_low(NORM_CONV, 0, slice(0, HALF), x_first_ready)
            start_unit_low(0, 1, 0)
            norm_low(NORM_CONV, 0, slice(HALF, S))
            start_unit_low(1, 2, 0)
            for m in range(1, KC):
                norm_low(NORM_CONV, m)
                if m == 2:
                    for u in range(BY_START):
                        start_unit_low(u, 3 + u, 1)
            dve.wait_ge(unit_high, 1)
            nc.vector.tensor_tensor(ring_l[:, BY_START, :], raw[:, BY_START, :], ring_h[:, BY_START, :].bitcast(F32),
                                    ALU.subtract).then_inc(unit_ready, 1)
            dve.wait_ge(small_landed, 16 * 2)
            norm_column(NORM_CONV, pdn[:, 0, 0:KC], 0, KC)
            norm_diag(0, KC)
            dve.wait_ge(rb_ready, 1)
            for f in range(KC):
                g, j = divmod(f, 2)
                adds = j == 1 and g >= 1
                conv_chunk(f, (lambda: down_adds(16 * (g - 1), 0, 2)) if adds else (lambda: None))
                if adds:
                    down_adds(16 * (g - 1), 2, 16)
            last_down(CONV_N + 16 * (CG - 1), NORM_FFN0)
            norm_column(NORM_FFN0, pdn[:, 0, 0:KC], 0, KC)
            norm_diag(0, KC)
            dve.wait_ge(rb_ready, 2)
            ffn(0)
            last_down(FFN_N[0] + 16 * (FG - 1), NORM_FOUR)
            norm_column(NORM_FOUR, pdn[:, 3, 256:256 + KC], 0, KC)

            def y_leaves(p):
                sine = pdn[:, 2 * (p % 2) + 1, :]
                y_even = rb.rearrange("p (j e) -> p j e", e=2)[:, :, 0]
                y_odd = rb.rearrange("p (j e) -> p j e", e=2)[:, :, 1]
                plus, minus = cst[:, P + 2:P + 3], cst[:, P + 3:P + 4]
                dve.wait_ge(y_cos, p + 1)
                for sign, even, odd in ((plus, y_even[:, 2 * Q - 1:Q:-1], y_odd[:, 2 * Q - 1:Q - 1:-1]),
                                        (minus, y_even[:, 1:Q], y_odd[:, 0:Q])):
                    nc.vector.scalar_tensor_tensor(even, sine[:, 1:Q], sign, y_even[:, 1:Q], ALU.mult, ALU.add)
                    nc.vector.scalar_tensor_tensor(odd, sine[:, Q:2 * Q], sign, y_odd[:, 0:Q], ALU.mult, ALU.add)
                nc.vector.tensor_copy(rb[:, S // 2:S // 2 + 1], sine[:, 0:1]).then_inc(y_made, 1)

            def evacuate(g):
                dve.wait_ge(z_done, 2 * g + 2)
                nc.vector.tensor_tensor(
                    of_group(t_b, g), computed(feature_banks(g), 4, 8),
                    rcol[:, 4:8].rearrange("p (c w e) -> p c w e", w=1, e=1).to_broadcast([P, 4, 2, E]),
                    ALU.mult).then_inc(z_hi, 1)

            dve.wait_ge(edge_zero, 2)
            evacuate(0)
            for p in range(PAIRS):
                evacuate(2 * p + 1)
                dve.wait_ge(z_hi, 2 * p + 2)
                dve.wait_ge(z_lo, 2 * p + 2)
                nc.vector.tensor_tensor(acc, t_a[:], t_b[:], ALU.add).then_inc(plus_made, 1)
                nc.vector.tensor_tensor(t_a[:], t_a[:], t_b[:], ALU.subtract).then_inc(minus_made, 1)
                dve.wait_ge(plus_made, p + 1)
                dve.wait_ge(plus_high, p + 1)
                slot = 2 * (p % 2)
                nc.vector.tensor_tensor(mid_l[:, slot, :], acc, mid_h[:, slot, :].bitcast(F32),
                                        ALU.subtract).then_inc(fold_ready, 1)
                dve.wait_ge(minus_made, p + 1)
                dve.wait_ge(minus_high, p + 1)
                nc.vector.tensor_tensor(mid_l[:, slot + 1, :], t_a[:], mid_h[:, slot + 1, :].bitcast(F32),
                                        ALU.subtract).then_inc(fold_ready, 1)
                if p < PAIRS - 1:
                    evacuate(2 * p + 2)
                if p:
                    y_leaves(p - 1)
                dve.wait_ge(fold_ready, 2 * p + 2)
                for mid, edge in ((mid_h, edge_h), (mid_l, edge_l)):
                    src = mid[:, slot:slot + 2, :].bitcast(F32).rearrange("p f (c n) -> p f c n", c=4)
                    dst = edge[:, 0:E].rearrange("p (f c o q) -> p f c o q", f=2, c=4, o=2)
                    last = nc.vector.tensor_copy(dst[:, :, :, :, p], src[:, :, :, P:2 * P:E])
                last.then_inc(edge_ready, 1)
            dve.wait_ge(edge_taken, 1)
            nc.vector.tensor_copy(t_b[0:KC, S - 1:S // 2:-1], t_b[0:KC, 1:S // 2]).then_inc(edge_made, 1)
            dve.wait_ge(edge_made, 1)
            dve.wait_ge(edge_high, 1)
            nc.vector.tensor_tensor(mid_l[0:KC, 0, :], t_b[0:KC, :], mid_h[0:KC, 0, :].bitcast(F32),
                                    ALU.subtract).then_inc(edge_low, 1)
            y_leaves(PAIRS - 1)
            for k in (KC - 2, KC - 1):
                dve.wait_ge(y_high, k + 1)
                dve.wait_ge(y_made, PAIRS)
                nc.vector.tensor_tensor(xs_l[:, k, :], wide[:, S:0:-1] if k % 2 else rb,
                                        xs_h[:, k, :].bitcast(F32), ALU.subtract).then_inc(y_last, 1)
            for m in range(KC):
                q = FOUR_Q + m
                if m == KC - 1:
                    for k in range(KC - 1):
                        norm_low(NORM_FFN1, k)
                dve.wait_ge(in_done, q + 1)
                nc.vector.tensor_tensor(res[:, m, :], in_pair(q).rearrange("p b n -> p (b n)"),
                                        res[:, m, :], ALU.add).then_inc(in_free, 1)
            norm_low(NORM_FFN1, KC - 1)
            norm_column(NORM_FFN1, pdn[:, 0, 0:KC], 0, KC)
            norm_diag(0, KC)
            dve.wait_ge(rb_ready, 3)
            ffn(1)
            def final_adds(first, end):
                for n in range(first, end):
                    h, m = divmod(n, KC)
                    cols = half_cols(h)
                    dve.wait_ge(down_done, FFN_N[1] + 16 * (FG - 1) + n + 1)
                    nc.vector.tensor_tensor(res[:, m, cols], pdn[:, n % BANKS, :],
                                            res[:, m, cols], ALU.add).then_inc(down_added, 1)

            def final_gains(h):
                for m in range(FINAL_DVE, KC):
                    dve.wait_ge(sq_done, (NORM_FINAL + h) * KC + m + 1)
                    nc.vector.tensor_scalar(res[:, m, half_cols(h)], res[:, m, half_cols(h)],
                                            gains[:, NORM_FINAL, m:m + 1], None, ALU.mult).then_inc(gained, 1)

            def final_scale(h, first, end):
                dve.wait_ge(rb_ready, 4 + h)
                cols = half_cols(h)
                for m in range(first, end):
                    nc.vector.scalar_tensor_tensor(res[:, m, cols], res[:, m, cols], gains[:, NORM_FINAL, m:m + 1],
                                                   rb[:, cols], ALU.mult, ALU.mult).then_inc(scaled[0], 1)

            def final_column(h):
                first, end = FINAL_HALVES[h]
                norm_column(NORM_FINAL + h, final_sums(h)[:, 0:end - first], first, end)
                norm_diag(first, end)

            final_adds(0, 12)
            final_column(0)
            final_gains(0)
            final_adds(12, 16)
            final_scale(0, 0, 5)
            final_column(1)
            final_gains(1)
            final_scale(0, 5, FINAL_DVE)
            final_scale(1, 0, FINAL_DVE)

        @block.tensor
        def _(pe):

            def passes(w_h, w_l, x_h, x_l):
                return ((w_h, x_h), (w_l, x_h), (w_h, x_l))

            def project_chunk(slot, pair, k, frees, signal=None, before_half=None):
                w = slice(k * P, (k + 1) * P)
                for h in range(2):
                    if before_half is not None:
                        before_half(h)
                    cols = slice(h * HALF, (h + 1) * HALF)
                    for i, (st, mv) in enumerate(passes(ring_h[:, slot, w], ring_l[:, slot, w],
                                                        xs_h[:, k, cols], xs_l[:, k, cols])):
                        last = nc.tensor.matmul(pair[:, h, :], st, mv,
                                                start=k == 0 and i == 0, stop=k == KC - 1 and i == 2)
                        if 3 * h + i < frees:
                            last.then_inc(unit_used, 1)
                if signal is not None:
                    last.then_inc(signal, 1)

            def project(u, slot_of, q, pair, before_chunk=None, spent=None):
                pe.wait_ge(unit_ready, u + (1 - BY_START))
                if not isinstance(q, int) or q > 2:
                    pe.wait_ge(in_free, q - 1)
                for k in range(KC):
                    if before_chunk is not None:
                        before_chunk(k)
                    project_chunk(slot_of % RING, pair, k, int(k == 0), in_done if k == KC - 1 else spent)

            def down(u, slot_of, a, base, odd, banks=range(16), halves_outer=False):
                if banks[0] == 0:
                    pe.wait_ge(unit_ready, u + (2 - BY_START))
                    pe.wait_ge(mid_ready, a + 2)
                for n in banks:
                    h, m = divmod(n, KC) if halves_outer else (n % 2, n // 2)
                    if not isinstance(base, int) or base + n >= BANKS:
                        pe.wait_ge(down_added, base + (n - (BANKS - 1)))
                    w, cols = slice(m * P, (m + 1) * P), half_cols(h)
                    for j in range(2):
                        slot, mid = (slot_of + j) % RING, 2 * (odd % 2) + j
                        for i, (st, mv) in enumerate(passes(ring_h[:, slot, w], ring_l[:, slot, w],
                                                            mid_h[:, mid, cols], mid_l[:, mid, cols])):
                            last = nc.tensor.matmul(pdn[:, n % BANKS, :], st, mv,
                                                    start=j == 0 and i == 0, stop=j == 1 and i == 2)
                            if n == 0 and j == 0 and i == 0:
                                last.then_inc(unit_used, 1)
                        if n == 15 and j == 0:
                            last.then_inc(unit_used, 1)
                    last.then_inc(down_done, 1)

            def column_sums(k, dst, c0, c1):
                pe.wait_ge(acc_done, adds_before(k + 1))
                parts = [acc]
                if ADDS[k] < KC - 1:
                    pe.wait_ge(sq_done, (k + 1) * KC)
                    parts.append(t_a)
                for j in range(c0, c1):
                    for part in parts:
                        last = nc.tensor.matmul(dst[:, j - c0:j - c0 + 1], part[:, j * P:(j + 1) * P],
                                                ones[:, 0:1], start=part is acc, stop=part is parts[-1])
                last.then_inc(colsum_done, 1)

            def spread(k, dst, c0, c1):
                pe.wait_ge(diag_done, k)
                for b in range((c1 - c0) * P // HALF):
                    cols = slice(c0 * P + b * HALF, c0 * P + (b + 1) * HALF)
                    last = nc.tensor.matmul(dst[:, b, :], ones[:], t_a[:, cols], start=True, stop=True)
                last.then_inc(bcast_done, 1)

            def first_two(norm, spread_k, u, q):
                project(u, u, q, in_pair(q), lambda k: pe.wait_ge(xs_ready, norm * KC + k + 1))
                column_sums(norm, pdn[:, 0, :], 0, KC)
                project(u + 1, u + 1, q + 1, in_pair(q + 1),
                        lambda k: spread(spread_k, pdn[:, 0:2, :], 0, KC) if k == 4 else None)

            def ffn(layer, norm, spread_k, last_banks):
                U, Q, N, A = FFN_U[layer], FFN_Q[layer], FFN_N[layer], FFN_A[layer]
                first_two(norm, spread_k, U, Q)
                project(U + 2, U + 2, Q + 2, in_pair(Q + 2))
                project(U + 3, U + 3, Q + 3, in_pair(Q + 3))
                with pe.Fori(0, (FG - 1) // 2) as i:
                    for odd in (1, 2):
                        g = i * 2 + odd
                        for j in range(4):
                            project(ffn_in_unit(layer, g) + j, U - 2 + 6 * odd + j, g * 4 + (Q + j),
                                    pin[:, 2 * (j % 2):2 * (j % 2) + 2, :])
                        down(ffn_down_unit(layer, g - 1), U + 2 + 6 * odd, i * 4 + (A + 2 * (odd - 1)),
                             i * 32 + (N + 16 * (odd - 1)), odd - 1)
                last = U + 3 * FC - 2
                last_banks(last, A + FC - 2, N + 16 * (FG - 1), FG - 1)

            pe.wait_ge(ones_set, 1)
            def first_chunk(h):
                if h == 0:
                    pe.wait_ge(x_first_ready, 1)
                else:
                    pe.wait_ge(xs_ready, 1)

            for u, k in start_steps():
                if k in (0, 4):
                    pe.wait_ge(start_ready, u + 1 + k // 2)
                if u == 0 and k:
                    pe.wait_ge(xs_ready, k + 1)
                project_chunk(u, in_pair(u), k, int((u, k) == (1, KC - 2)), in_done if k == KC - 1 else None,
                              first_chunk if (u, k) == (0, 0) else None)

            def start_norm(k):
                if k == 0:
                    column_sums(NORM_CONV, pdn[:, 0, :], 0, KC)
                if k == 4:
                    spread(1, pdn[:, 0:2, :], 0, KC)

            for g in range(CG):
                for j in range(6):
                    if g or j >= 2:
                        u, q = conv_in_unit(g) + j, 6 * g + j
                        project(u, u, q, in_pair(q), start_norm if q == 2 else None)
                if g:
                    down(conv_down_unit(g - 1), conv_down_unit(g - 1), CONV_A + 2 * (g - 1), 16 * (g - 1), g - 1)
            down(conv_down_unit(CG - 1), conv_down_unit(CG - 1), CONV_A + KC - 2, 16 * (CG - 1), CG - 1)

            ffn(0, NORM_FFN0, 2, lambda u, a, base, odd: down(u, u, a, base, odd))

            def feature_transform(g, first=0, end=KC):
                pe.wait_ge(xs_ready, NORM_FOUR * KC + g + 1)
                banks = feature_banks(g)
                for c in range(first, end):
                    before = 0 if g == 2 else g - 1
                    if g >= 2 and c == 0:
                        pe.wait_ge(z_lo, before + 1)
                    if g >= 2 and c == 4:
                        pe.wait_ge(z_hi, before + 1)
                    if g == 1 and c % 2 == 0:
                        pe.wait_ge(down_added, FFN_N[1] - BANKS + c // 2 + 1)
                    rows = slice(c * P, (c + 1) * P)
                    z_h, z_l = xs_h[:, g, rows], xs_l[:, g, rows]
                    high, low = feat[:, 0:4 * E], feat[:, E:5 * E]
                    for i, (st, mv) in enumerate(passes(z_h, z_l, high, low)):
                        last = nc.tensor.matmul(banks[:, c // 2, (c % 2) * 256:(c % 2 + 1) * 256], st, mv,
                                                start=i == 0, stop=i == 2)
                        if g == 0 and c == 0 and i == 0:
                            last.then_inc(unit_used, 1)
                    if c % 4 == 3:
                        last.then_inc(z_done, 1)

            def alternating_sum(out, z_h, z_l, stop):
                for c in range(4):
                    for i, z in enumerate((z_h(c), z_l(c))):
                        nc.tensor.matmul(out, z, alt[:], start=stop and c == 0 and i == 0,
                                         stop=stop and c == 3 and i == 1)

            def position_transform(p, fold):
                if p >= 2 and fold == 0:
                    pe.wait_ge(y_made, p - 1)
                pe.wait_ge(fold_ready, 2 * p + fold + 1)
                mid = 2 * (p % 2) + fold
                for wave in range(2):
                    table = (FOUR_U + 2 * fold + wave) % RING
                    out = pdn[:, 2 * (p % 2) + wave, fold * 256:(fold + 1) * 256]
                    for c in range(4):
                        if fold == 0 and wave == 1 and c == 1:
                            alternating_sum(out[:, 0:2], lambda b: mid_h[:, mid, b * 256:b * 256 + P],
                                            lambda b: mid_l[:, mid, b * 256:b * 256 + P], False)
                        st = slice(c * 256 + wave * P, c * 256 + (wave + 1) * P)
                        mv = slice(c * 256, (c + 1) * 256)
                        for i, (z, w) in enumerate(passes(mid_h[:, mid, st], mid_l[:, mid, st],
                                                          ring_h[:, table, mv], ring_l[:, table, mv])):
                            last = nc.tensor.matmul(out, z, w, start=c == 0 and i == 0,
                                                    stop=c == 3 and i == 2)
                if fold == 1:
                    last.then_inc(y_done, 1)

            def edge_transform():
                pe.wait_ge(edge_ready, PAIRS)
                pe.wait_ge(z_lo, KC)
                def window(edge, fold, c):
                    at = (4 * fold + c) * KC
                    return edge[:, at:at + EDGE_COLS]
                alternating_sum(pin[0:EDGE_COLS, 1, 0:2], lambda c: window(edge_h, 0, c),
                                lambda c: window(edge_l, 0, c), True)
                for fold in range(2):
                    table = (FOUR_U + 2 * fold) % RING
                    for c in range(4):
                        mv = slice(c * 256, (c + 1) * 256)
                        for i, (z, w) in enumerate(passes(window(edge_h, fold, c), window(edge_l, fold, c),
                                                          ring_h[:, table, mv], ring_l[:, table, mv])):
                            last = nc.tensor.matmul(pin[0:EDGE_COLS, 0, fold * 256:(fold + 1) * 256], z, w,
                                                    start=c == 0 and i == 0, stop=c == 3 and i == 2)
                last.then_inc(edge_done, 1)

            pe.wait_ge(feat_ready, 1)
            pe.wait_ge(feat_pad, 1)
            pe.wait_ge(alt_ready, 1)
            feature_transform(0)
            feature_transform(1, 0, KC - 1)
            column_sums(NORM_FOUR, pdn[:, 3, 256:], 0, KC)
            pe.wait_ge(stat_done, NORM_FOUR + 1)
            feature_transform(1, KC - 1)
            pe.wait_ge(unit_ready, FOUR_U + 4 - BY_START)
            W = FOUR_U + 4

            def w_chunks(m, chunks, frees=0):
                for k in chunks:
                    if k < KC - 2:
                        pe.wait_ge(y_ready, k + 1)
                    else:
                        pe.wait_ge(y_last, k + 3 - KC)
                    project_chunk((W + m) % RING, in_pair(FOUR_Q + m), k, frees,
                                  in_done if k == KC - 1 else None)
                    frees = 0

            for p in range(PAIRS - 1):
                for fold in range(2):
                    feature_transform(2 * p + 2 + fold)
                    position_transform(p, fold)
            pe.wait_ge(unit_ready, W + 2 - BY_START)
            pe.wait_ge(z_hi, KC)
            w_chunks(1, (0, 2))
            position_transform(PAIRS - 1, 0)
            edge_transform()
            position_transform(PAIRS - 1, 1)
            pe.wait_ge(edge_taken, 1)
            w_chunks(0, (0, 2, 4), 4)
            w_chunks(1, (4,))
            pe.wait_ge(edges_landed, 4 * 16)
            for m in range(2):
                w_chunks(m, (1, 3, 5))
            for m in range(2):
                w_chunks(m, (6,))
            pe.wait_ge(last_edge_landed, 4 * 16)
            w_chunks(0, (7,))
            w_chunks(1, (7,), 1)
            for m in range(2, KC):
                project(W + m, W + m, FOUR_Q + m, in_pair(FOUR_Q + m),
                        spent=y_spent if m == KC - 1 else None)

            def last_banks(u, a, base, odd):
                def final_spread(h):
                    spread(NORM_FINAL + h, final_spread_bank(h).rearrange("p (b n) -> p b n", b=1), *FINAL_HALVES[h])

                down(u, u, a, base, odd, range(0, 12), True)
                column_sums(NORM_FINAL, final_sums(0), *FINAL_HALVES[0])
                down(u, u, a, base, odd, range(12, 14), True)
                final_spread(0)
                down(u, u, a, base, odd, range(14, 16), True)
                column_sums(NORM_FINAL + 1, final_sums(1), *FINAL_HALVES[1])
                final_spread(1)

            ffn(1, NORM_FFN1, 3, last_banks)


def dft_tables():
    import numpy as np

    s = np.arange(S // 2)[:, None]
    j = np.arange(S // 4)[None, :]
    even = 2 * np.pi * ((s * 2 * j) % S) / S
    odd = 2 * np.pi * ((s * (2 * j + 1)) % S) / S
    waves = [np.cos(even), np.sin(even), np.cos(odd), np.sin(odd)]
    waves[1][:, 0] = 0.0
    seq = np.stack([w.reshape(4, P, S // 4).transpose(1, 0, 2).reshape(P, D) for w in waves]) * S ** -0.5
    d, e = np.arange(P)[:, None], np.arange(E)[None, :]
    turn = 2 * np.pi * ((d * e) % P) / P
    feat = np.concatenate([np.cos(turn), np.sin(turn)], axis=1) * P ** -0.5
    sign = 1.0 - 2.0 * (np.arange(P) % 2)
    feat[:, E] = sign * P ** -0.5
    cst = np.zeros((P, P + 4))
    cst[:, 0:P] = np.eye(P)
    cst[:, P] = sign * S ** -0.5
    cst[:, P + 2] = np.arange(P) % E != 0
    cst[:, P + 3] = -cst[:, P + 2]
    return [a.astype(np.float32) for a in (seq.reshape(4 * P, D), feat, cst)]


def fourier_rows():
    f = [e for e in range(E)]
    r = [E] + [P - e for e in range(1, E)]
    return [g * P + e for p in range(PAIRS) for rows in (f, r) for g in (2 * p, 2 * p + 1) for e in rows]


def kernel(x, conv_w_in, conv_k, conv_w_out, fourier_w_out, mix_norm_g, ffn_norm_g, ffn_w_gate, ffn_w_up,
           ffn_w_down, final_norm_g):
    import numpy as np
    import concourse.bacc as bacc
    from concourse.bass_utils import run_bass_kernel_spmd

    def column_units(w):
        w = np.asarray(w)
        n = w.shape[-1] // P
        w = w.reshape(-1, KC, P, n, P).transpose(0, 3, 2, 1, 4)
        return np.ascontiguousarray(w.reshape(-1, D))

    gains = [mix_norm_g[0], ffn_norm_g[0], mix_norm_g[1], ffn_norm_g[1], final_norm_g]
    gains = np.stack([np.asarray(g) for g in gains]).reshape(5, KC, P).transpose(2, 0, 1)
    taps = np.asarray(conv_k)[0].reshape(3, KC, P).transpose(2, 0, 1)
    seq, feat, cst = dft_tables()
    arrays = {
        "xT": np.ascontiguousarray(np.asarray(x)[0].T),
        "w_in": column_units(conv_w_in),
        "w_conv": np.ascontiguousarray(np.asarray(conv_w_out)[0]),
        "w_four": column_units(np.asarray(fourier_w_out)[:, fourier_rows(), :]),
        "w_gate": column_units(ffn_w_gate),
        "w_up": column_units(ffn_w_up),
        "w_down": np.ascontiguousarray(np.asarray(ffn_w_down).reshape(2 * FF, D)),
        "gains": np.ascontiguousarray(gains),
        "taps": np.ascontiguousarray(taps),
        "seq": seq,
        "feat": feat,
        "cst": cst,
    }
    nc = bacc.Bacc("TRN2", target_bir_lowering=False, num_devices=1)
    args = [nc.dram_tensor(name + "_dram", a.shape, mybir.dt.float32, kind="ExternalInput").ap()
            for name, a in arrays.items()]
    out = nc.dram_tensor("out_dram", (D, S), mybir.dt.float32, kind="ExternalOutput").ap()
    build(nc, *args, out)
    result = run_bass_kernel_spmd(nc, [{name + "_dram": a for name, a in arrays.items()}], core_ids=[0])
    return np.ascontiguousarray(result.results[0]["out_dram"].T).reshape(1, S, D)
```
